# Optimizing a Trainium2 kernel written in Bass

```python
import jax
import jax.numpy as jnp
from jax import lax
import numpy as np

D_MODEL = 1024
BATCH = 1
SEQ = 512
DEPTH = 2

GRID_W = 64
CTX_LEN = 256
HEAD_DIM = 64
ATTN_HEADS = 8
ATTN_KV_HEADS = 2
ATTN_REP = ATTN_HEADS // ATTN_KV_HEADS
Q_BLOCK = 128
ROPE_THETA = 10000.0
ROPE_AXIS_DIM = HEAD_DIM // 2
HG_HEADS = 4
HG_DK = 64
HG_DV = 64
ML_HEADS = 4
ML_DK = 64
ML_DV = 64
ML_CONV = 3
CHUNK = 64
FF_DIM = 4 * D_MODEL
N_MOD = 6
EPS = 1e-6
ATTN_W = ATTN_HEADS * HEAD_DIM
KV_W = ATTN_KV_HEADS * HEAD_DIM
HG_W = HG_HEADS * HG_DK
HG_VW = HG_HEADS * HG_DV
ML_W = ML_HEADS * ML_DK
ML_VW = ML_HEADS * ML_DV
MIX_WIDTH = ATTN_W + HG_VW + ML_VW
IN_SIZES = (ATTN_W, KV_W, KV_W,
            HG_W, HG_VW, HG_W, HG_W, HG_VW,
            ML_W, ML_W, ML_VW, ML_VW, ML_HEADS, ML_HEADS, ML_HEADS, ML_HEADS)
N_IN = sum(IN_SIZES)
ML_FGATE_FWD = 14
ML_FGATE_BWD = 15

kernel_name = 'hybrid_parallel_heads_dit_block'

def split_columns(p):
    idx = np.cumsum(np.array(IN_SIZES))[:-1].tolist()
    return jnp.split(p, idx, axis=-1)

def rmsnorm(x, g):
    xf = x.astype(jnp.float32)
    y = xf * lax.rsqrt(jnp.mean(xf * xf, axis=-1, keepdims=True) + EPS)
    return (y * g.astype(jnp.float32)).astype(x.dtype)

def modulate(x, shift, scale):
    return x * (1 + scale) + shift

def to_heads(x, h):
    b, n, _ = x.shape
    return x.reshape(b, n, h, -1).transpose(0, 2, 1, 3)

def from_heads(x):
    b, h, n, d = x.shape
    return x.transpose(0, 2, 1, 3).reshape(b, n, h * d)

def rotate_pairs(x, ang):
    half = x.shape[-1] // 2
    cos = jnp.cos(ang)[:, None, :].astype(x.dtype)
    sin = jnp.sin(ang)[:, None, :].astype(x.dtype)
    x1, x2 = x[..., :half], x[..., half:]
    return jnp.concatenate([x1 * cos - x2 * sin, x2 * cos + x1 * sin], axis=-1)

def rope_2d(x, ang_row, ang_col):
    return jnp.concatenate([rotate_pairs(x[..., :ROPE_AXIS_DIM], ang_row),
                            rotate_pairs(x[..., ROPE_AXIS_DIM:], ang_col)], axis=-1)

def sdpa(q, k, v):
    s = jnp.einsum('bgrtd,bgmd->bgrtm', q, k).astype(jnp.float32) * (HEAD_DIM ** -0.5)
    p = jax.nn.softmax(s, axis=-1).astype(v.dtype)
    return jnp.einsum('bgrtm,bgmd->bgrtd', p, v)

def attention_mixer(lat, ctx, gq, gk, ang_row, ang_col, need_ctx):
    q, k, v = lat
    qc, kc, vc = ctx
    bsz, n, _ = q.shape
    nc = qc.shape[1]

    def split_heads(t, h):
        return t.reshape(t.shape[0], t.shape[1], h, HEAD_DIM)

    q = rope_2d(rmsnorm(split_heads(q, ATTN_HEADS), gq), ang_row, ang_col)
    k = rope_2d(rmsnorm(split_heads(k, ATTN_KV_HEADS), gk), ang_row, ang_col)
    v = split_heads(v, ATTN_KV_HEADS)
    kc = rmsnorm(split_heads(kc, ATTN_KV_HEADS), gk).transpose(0, 2, 1, 3)
    vc = split_heads(vc, ATTN_KV_HEADS).transpose(0, 2, 1, 3)
    keys = jnp.concatenate([kc, k.transpose(0, 2, 1, 3)], axis=2)
    vals = jnp.concatenate([vc, v.transpose(0, 2, 1, 3)], axis=2)
    nb = n // Q_BLOCK
    qb = q.reshape(bsz, nb, Q_BLOCK, ATTN_KV_HEADS, ATTN_REP, HEAD_DIM).transpose(1, 0, 3, 4, 2, 5)
    ob = lax.map(lambda qi: sdpa(qi, keys, vals), qb)
    out = ob.transpose(1, 0, 4, 2, 3, 5).reshape(bsz, n, ATTN_W)
    if not need_ctx:
        return out, None
    qcg = rmsnorm(split_heads(qc, ATTN_HEADS), gq)
    qcg = qcg.reshape(bsz, nc, ATTN_KV_HEADS, ATTN_REP, HEAD_DIM).transpose(0, 2, 3, 1, 4)
    oc = sdpa(qcg, kc, vc).transpose(0, 3, 1, 2, 4).reshape(bsz, nc, ATTN_W)
    return out, oc

def chunk_scan(step, init, xs):
    bsz, h, n = xs[0].shape[:3]
    nch = n // CHUNK
    xs_c = tuple(jnp.moveaxis(a.reshape((bsz, h, nch, CHUNK) + a.shape[3:]), 2, 0) for a in xs)
    state, out = lax.scan(step, init, xs_c)
    out = jnp.moveaxis(out, 0, 2)
    return out.reshape((bsz, h, n) + out.shape[4:]), state

def run_direction(step, init, ctx_xs, lat_xs, reverse):
    if reverse:
        ctx_xs = tuple(jnp.flip(a, axis=2) for a in ctx_xs)
        lat_xs = tuple(jnp.flip(a, axis=2) for a in lat_xs)
    out_c, state_c = chunk_scan(step, init, ctx_xs)
    out_l, _ = chunk_scan(step, state_c, lat_xs)
    if reverse:
        out_c, out_l = jnp.flip(out_c, axis=2), jnp.flip(out_l, axis=2)
    return out_c, out_l

def hgrn_step(S, xs):
    q, k, lf, v = xs
    L = q.shape[2]
    tri = jnp.tril(jnp.ones((L, L), bool))[:, :, None]
    b = jnp.cumsum(lf, axis=2)
    diff = b[:, :, :, None, :] - b[:, :, None, :, :]
    dec = jnp.where(tri, jnp.exp(jnp.where(tri, diff, 0.0)), 0.0)
    scores = jnp.einsum('bhtsk,bhtk,bhsk->bhts', dec, q, k)
    o = jnp.einsum('bhts,bhsv->bhtv', scores, v) + jnp.einsum('bhtk,bhkv->bhtv', q * jnp.exp(b), S)
    b_last = b[:, :, -1:, :]
    S_new = jnp.exp(b_last[:, :, 0, :, None]) * S + jnp.einsum('bhsk,bhsv->bhkv', k * jnp.exp(b_last - b), v)
    return S_new, o

def hgrn2_mixer(lat, ctx, lb_fwd, lb_bwd, g_norm, need_ctx):
    def prep(q, i, zf, zb):
        q = to_heads(q, HG_HEADS).astype(jnp.float32)
        v = to_heads(i, HG_HEADS).astype(jnp.float32)

        def gate(z, lb):
            lb = lb.astype(jnp.float32).reshape(HG_HEADS, 1, HG_DK)
            f = lb + (1.0 - lb) * jax.nn.sigmoid(to_heads(z, HG_HEADS).astype(jnp.float32))
            return 1.0 - f, jnp.log(f)

        k_f, lf_f = gate(zf, lb_fwd)
        k_b, lf_b = gate(zb, lb_bwd)
        return (q, k_f, lf_f, v), (q, k_b, lf_b, v)

    def readout(o, g):
        o = rmsnorm(o.transpose(0, 2, 1, 3), g_norm)
        return (o.reshape(g.shape) * jax.nn.silu(g.astype(jnp.float32))).astype(g.dtype)

    lat_f, lat_b = prep(*lat[:4])
    ctx_f, ctx_b = prep(*ctx[:4])
    s0 = jnp.zeros((lat[0].shape[0], HG_HEADS, HG_DK, HG_DV), jnp.float32)
    oc_f, o_f = run_direction(hgrn_step, s0, ctx_f, lat_f, False)
    oc_b, o_b = run_direction(hgrn_step, s0, ctx_b, lat_b, True)
    out = readout(o_f + o_b, lat[4])
    oc = readout(oc_f + oc_b, ctx[4]) if need_ctx else None
    return out, oc

def mlstm_step(state, xs):
    C, n, m = state
    q, k, v, ig, lf = xs
    L = q.shape[2]
    tri = jnp.tril(jnp.ones((L, L), bool))
    b = jnp.cumsum(lf, axis=-1)
    log_d = jnp.where(tri, b[..., :, None] - b[..., None, :] + ig[..., None, :], -jnp.inf)
    m_t = jnp.maximum(b + m[..., None], jnp.max(log_d, axis=-1))
    d = jnp.exp(log_d - m_t[..., None])
    g = jnp.exp(b + m[..., None] - m_t)
    s = jnp.einsum('bhtd,bhsd->bhts', q, k) * d
    num = g[..., None] * jnp.einsum('bhtk,bhkv->bhtv', q, C) + jnp.einsum('bhts,bhsv->bhtv', s, v)
    den = g * jnp.einsum('bhtk,bhk->bht', q, n) + jnp.sum(s, axis=-1)
    h = num / jnp.maximum(jnp.abs(den), jnp.exp(-m_t))[..., None]
    b_last = b[..., -1]
    log_e = b_last[..., None] - b + ig
    m_new = jnp.maximum(b_last + m, jnp.max(log_e, axis=-1))
    ke = k * jnp.exp(log_e - m_new[..., None])[..., None]
    g_c = jnp.exp(b_last + m - m_new)
    C_new = g_c[..., None, None] * C + jnp.einsum('bhsk,bhsv->bhkv', ke, v)
    n_new = g_c[..., None] * n + jnp.sum(ke, axis=2)
    return (C_new, n_new, m_new), h

def conv_centred(x, w):
    taps = w.shape[0]
    pad = taps // 2
    n = x.shape[1]
    xp = jnp.pad(x, ((0, 0), (pad, pad), (0, 0)))
    y = xp[:, 0:n] * w[0]
    for j in range(1, taps):
        y = y + xp[:, j:j + n] * w[j]
    return y

def mlstm_mixer(lat, ctx, conv_w, need_ctx):
    f32 = jnp.float32

    def prep(q, k, v, ig_f, ig_b, fg_f, fg_b):
        qk = jax.nn.silu(conv_centred(jnp.concatenate([q, k], axis=-1), conv_w))
        q, k = jnp.split(qk, 2, axis=-1)
        q = to_heads(q, ML_HEADS).astype(f32)
        k = to_heads(k, ML_HEADS).astype(f32) * (ML_DK ** -0.5)
        v = to_heads(v, ML_HEADS).astype(f32)
        heads = lambda t: t.astype(f32).transpose(0, 2, 1)
        return ((q, k, v, heads(ig_f), jax.nn.log_sigmoid(heads(fg_f))),
                (q, k, v, heads(ig_b), jax.nn.log_sigmoid(heads(fg_b))))

    q, k, v, o, ig_f, ig_b, fg_f, fg_b = lat
    lat_f, lat_b = prep(q, k, v, ig_f, ig_b, fg_f, fg_b)
    ctx_f, ctx_b = prep(ctx[0], ctx[1], ctx[2], *ctx[4:])
    bsz = q.shape[0]
    init = (jnp.zeros((bsz, ML_HEADS, ML_DK, ML_DV), f32),
            jnp.zeros((bsz, ML_HEADS, ML_DK), f32),
            jnp.zeros((bsz, ML_HEADS), f32))
    hc_f, h_f = run_direction(mlstm_step, init, ctx_f, lat_f, False)
    hc_b, h_b = run_direction(mlstm_step, init, ctx_b, lat_b, True)
    out = (jax.nn.sigmoid(o.astype(f32)) * from_heads(h_f + h_b)).astype(o.dtype)
    if not need_ctx:
        return out, None
    oc = (jax.nn.sigmoid(ctx[3].astype(f32)) * from_heads(hc_f + hc_b)).astype(ctx[3].dtype)
    return out, oc

def sq_relu_mlp(u, w1, w2):
    return jnp.square(jax.nn.relu(u @ w1)) @ w2

def setup_inputs(seed: int = 0) -> dict:
    key = jax.random.key(seed)
    ks = jax.random.split(key, 18)
    f32 = jnp.float32
    nrm = lambda k, shape, s: jax.random.normal(k, shape, f32) * s
    starts = np.concatenate([[0], np.cumsum(np.array(IN_SIZES))[:-1]])
    fg_off = np.zeros((N_IN,), np.float32)
    for idx in (ML_FGATE_FWD, ML_FGATE_BWD):
        fg_off[starts[idx]:starts[idx] + ML_HEADS] = np.linspace(3.0, 6.0, ML_HEADS)
    return {
        'x': nrm(ks[0], (BATCH, SEQ, D_MODEL), 1.0),
        'c': nrm(ks[1], (BATCH, D_MODEL), 1.0),
        'ctx': nrm(ks[2], (BATCH, CTX_LEN, D_MODEL), 1.0),
        'c_ctx': nrm(ks[3], (D_MODEL,), 1.0),
        'w_mod': nrm(ks[4], (DEPTH, D_MODEL, N_MOD * D_MODEL), 0.5 * D_MODEL ** -0.5),
        'b_mod': nrm(ks[5], (DEPTH, N_MOD * D_MODEL), 0.02),
        'norm_mix': 1.0 + nrm(ks[6], (DEPTH, D_MODEL), 0.02),
        'norm_ffn': 1.0 + nrm(ks[7], (DEPTH, D_MODEL), 0.02),
        'w_in': nrm(ks[8], (DEPTH, D_MODEL, N_IN), D_MODEL ** -0.5),
        'b_in': nrm(ks[9], (DEPTH, N_IN), 0.02) + jnp.asarray(fg_off),
        'q_norm': 1.0 + nrm(ks[10], (DEPTH, HEAD_DIM), 0.02),
        'k_norm': 1.0 + nrm(ks[11], (DEPTH, HEAD_DIM), 0.02),
        'hg_lb': nrm(ks[12], (DEPTH, 2, HG_W), 0.1),
        'hg_norm': 1.0 + nrm(ks[13], (DEPTH, HG_DV), 0.02),
        'ml_conv': nrm(ks[14], (DEPTH, ML_CONV, 2 * ML_W), ML_CONV ** -0.5),
        'w_out': nrm(ks[15], (DEPTH, MIX_WIDTH, D_MODEL), MIX_WIDTH ** -0.5),
        'w_ff1': nrm(ks[16], (DEPTH, D_MODEL, FF_DIM), D_MODEL ** -0.5),
        'w_ff2': nrm(ks[17], (DEPTH, FF_DIM, D_MODEL), FF_DIM ** -0.5),
    }

def reference(x, c, ctx, c_ctx, w_mod, b_mod, norm_mix, norm_ffn, w_in, b_in, q_norm, k_norm,
              hg_lb, hg_norm, ml_conv, w_out, w_ff1, w_ff2):
    f32 = jnp.float32
    n = x.shape[1]
    ROWS = n // GRID_W
    inv_freq = ROPE_THETA ** (-jnp.arange(0, ROPE_AXIS_DIM, 2, dtype=f32) / ROPE_AXIS_DIM)
    row = jnp.repeat(jnp.arange(ROWS), GRID_W).astype(f32)
    col = (jnp.arange(n) % GRID_W).astype(f32)
    ang_row = row[:, None] * inv_freq[None, :]
    ang_col = col[:, None] * inv_freq[None, :]
    lbs = jnp.cumsum(jax.nn.softmax(hg_lb.astype(f32), axis=0), axis=0)
    lbs = lbs - lbs[:1]
    h, hc = x, ctx
    for l in range(DEPTH):
        need_ctx = l < DEPTH - 1
        mod = (jax.nn.silu(c) @ w_mod[l] + b_mod[l])[:, None, :]
        mod_c = jax.nn.silu(c_ctx) @ w_mod[l] + b_mod[l]
        sh1, sc1, g1, sh2, sc2, g2 = jnp.split(mod, N_MOD, axis=-1)
        csh1, csc1, cg1, csh2, csc2, cg2 = jnp.split(mod_c, N_MOD, axis=-1)
        u = modulate(rmsnorm(h, norm_mix[l]), sh1, sc1)
        uc = modulate(rmsnorm(hc, norm_mix[l]), csh1, csc1)
        p = split_columns(u @ w_in[l] + b_in[l])
        pc = split_columns(uc @ w_in[l] + b_in[l])
        a, ac = attention_mixer(p[0:3], pc[0:3], q_norm[l], k_norm[l], ang_row, ang_col, need_ctx)
        r, rc = hgrn2_mixer(p[3:8], pc[3:8], lbs[l, 0], lbs[l, 1], hg_norm[l], need_ctx)
        m, mc = mlstm_mixer(p[8:16], pc[8:16], ml_conv[l], need_ctx)
        h = h + g1 * (jnp.concatenate([a, r, m], axis=-1) @ w_out[l])
        h = h + g2 * sq_relu_mlp(modulate(rmsnorm(h, norm_ffn[l]), sh2, sc2), w_ff1[l], w_ff2[l])
        if need_ctx:
            hc = hc + cg1 * (jnp.concatenate([ac, rc, mc], axis=-1) @ w_out[l])
            hc = hc + cg2 * sq_relu_mlp(modulate(rmsnorm(hc, norm_ffn[l]), csh2, csc2), w_ff1[l], w_ff2[l])
    return h


_drawn_inputs = setup_inputs


def setup_inputs(seed=0):
    import zlib

    import numpy as np

    out = dict(_drawn_inputs(seed))
    spreads = {}
    factors = {'ctx': 2.956,
     'norm_mix': 4.978,
     'norm_ffn': 4.404,
     'q_norm': 8.0,
     'k_norm': 8.0,
     'hg_lb': 8.0,
     'hg_norm': 8.0}
    for name, (base, spread) in spreads.items():
        noise = np.random.default_rng([zlib.crc32(name.encode()), seed]).standard_normal(out[name].shape)
        drawn = base * np.exp(spread * noise) if base else spread * noise
        out[name] = jnp.asarray(drawn.astype(out[name].dtype))
    for name, factor in factors.items():
        out[name] = (out[name] * factor).astype(out[name].dtype)
    return out
```

```python
from contextlib import ExitStack

import numpy as np

import concourse.bass as bass
from concourse import mybir

F32 = mybir.dt.float32
F32R = mybir.dt.float32r
U8 = mybir.dt.uint8
ALU = mybir.AluOpType
ACT = mybir.ActivationFunctionType
AX = mybir.AxisListType

P = 128
D = 1024
DK = D // P
CTX = 256
LAT = 512
T = CTX + LAT
DEPTH = 2
HD = 64
C = 128
NC = T // C
EPS = 1e-6
N_IN = 3088
IN_TILES = 24
FF = 4096
FG = 4
SEGS = ((0, CTX), (CTX, LAT))
AQ, AK, AV, HQ, HV, HZ, HG, MQ, MK, MV, MO, GT = 0, 4, 5, 6, 8, 10, 14, 16, 18, 20, 22, 24
LEVELS = 7
ORDER = (tuple(range(NC)), (1, 0, 5, 4, 3, 2))
STEP = tuple(tuple(o.index(c) for c in range(NC)) for o in ORDER)

K_ID, K_ROT, K_COS, K_SIN, K_KZ, K_BLK, K_ONE, K_HM, K_MASK, K_SEL, K_PAIR = (
    0, 128, 256, 768, 1280, 1792, 1920, 2048, 2050, 2306, 3330)
K_N = 3842
V_BMOD, V_NMIX, V_NFFN, V_BIN, V_LB, V_CONV, V_QN, V_KN, V_HN, V_C = 0, 96, 112, 128, 176, 184, 208, 210, 212, 214
V_N = 230


def tables():
    k = np.zeros((P, K_N), np.float32)
    k[:, K_ID:K_ID + P] = np.eye(P)
    for base in range(0, P, 32):
        for i in range(16):
            k[base + 16 + i, K_ROT + base + i] = -1.0
            k[base + i, K_ROT + base + 16 + i] = 1.0
    half = HD // 2
    inv = (np.float32(10000.0) ** (-np.arange(0, half, 2, dtype=np.float32) / np.float32(half))).astype(np.float32)
    tok = np.arange(LAT)
    row = (tok // 64).astype(np.float32)[None, :] * inv[:, None]
    col = (tok % 64).astype(np.float32)[None, :] * inv[:, None]
    ang = np.concatenate([row, row, col, col] * 2, axis=0)
    k[:, K_COS:K_COS + LAT] = np.cos(ang)
    k[:, K_SIN:K_SIN + LAT] = np.sin(ang)
    for g in range(2):
        for par in range(2):
            for d in range(HD):
                k[64 * g + d, K_KZ + (2 * g + par) * P + 64 * par + d] = 1.0
    for b in range(2):
        k[64 * b:64 * b + 64, K_BLK + 64 * b:K_BLK + 64 * b + 64] = 1.0 / HD
        k[64 * b:64 * b + 64, K_HM + b] = 1.0
    k[:, K_ONE:K_ONE + P] = 1.0 / D
    s, t = np.arange(C)[:, None], np.arange(C)[None, :]
    k[:, K_MASK:K_MASK + C] = np.where(s <= t, 0.0, -1e30)
    k[:, K_MASK + C:K_MASK + 2 * C] = np.where(s >= t, 0.0, -1e30)
    for d in range(2):
        for h in range(4):
            k[32 * d + h, K_SEL + (4 * d + h) * P:K_SEL + (4 * d + h + 1) * P] = 1.0
        for tt in range(2):
            for par in range(2):
                at = K_PAIR + (2 * d + tt) * P + 64 * par
                k[32 * d + 2 * tt + par, at:at + 64] = 1.0
    m = np.zeros((P, LEVELS + 1, C), np.float32)
    m[:, 0] = s == t
    for lv in range(LEVELS):
        b = 2 << lv
        m[:, lv + 1] = (s // b == t // b) & (s // (b // 2) != t // (b // 2))
    return k, m



class Signal:

    def __init__(self, sem, per_layer=0):
        self.sem, self.per_layer = sem, per_layer

    def at(self, layer, n):
        return self.sem, layer * self.per_layer + n


def hybrid_dit_block(nc: bass.Bass, x, c, ctx_in, c_ctx, w_mod, b_mod, norm_mix, norm_ffn, w_in, b_in, q_norm, k_norm,
                     hg_lb, hg_norm, ml_conv, w_out, w_ff1, w_ff2, consts, level_masks, out):
    with ExitStack() as es:
        base = 16512
        slot = T
        W_H, W_U, W_P = 0, 8 * slot, 24 * slot
        W_RAW = 49 * slot
        W_HI, W_LO = W_RAW + 4096, W_RAW + 4096 + 2048
        W_K = W_LO + 2048
        W_M8 = W_K + K_N + 6
        W_X = W_M8 + 256

        def at(name, shape, word, dt=F32):
            return nc.alloc_sbuf_tensor_at(name, shape, dt, offset=base + 4 * word)

        def u_at(n):
            return W_U + n * slot

        def p_at(n):
            return W_P + n * slot

        H = at("residual", [P, DK, T], W_H)
        Uh = at("u_high", [P, DK, T], u_at(0), F32R)
        Ul = at("u_low", [P, DK, T], u_at(8), F32R)
        PT_ = at("projections", [P, 25, T], p_at(0))
        raw = at("weights_raw", [P, 4, DK, P], W_RAW)
        whi = at("weights_high", [P, 2, DK, P], W_HI, F32R)
        wlo = at("weights_low", [P, 2, DK, P], W_LO, F32R)
        K = at("constants", [P, K_N], W_K)
        M8 = at("level_masks", [P, LEVELS + 1, C], W_M8, U8)
        V = at("parameters", [P, V_N], W_X + 0)
        MOD = at("modulation", [P, DEPTH, 48, 2], W_X + 232)
        GAIN = at("norm_gains", [P, DEPTH, 2, DK, 2], W_X + 424)
        GB = at("gate_bias", [P, DEPTH], W_X + 488)
        LBT = at("lb_work", [P, 5, 4], W_X + 496)
        LB = at("lower_bounds", [P, DEPTH, 4], W_X + 520)
        LB1 = at("one_minus_lower_bounds", [P, DEPTH, 4], W_X + 528)
        EPST = at("epsilon", [P, 2], W_X + 536)
        GCOL = at("gate_columns", [P, NC, 3, 2, 4], W_X + 544)
        GC = at("chunk_decays", [P, 4, NC], W_X + 688)
        MPREV = at("max_before_chunk", [64, NC], W_X + 712)
        CS = at("silu_c", [P, DK, 2], W_X + 720)
        NEGM = at("minus_row_max", [P, 8], W_X + 736)
        DEN = at("denominators", [P, 2, 2, 4], W_X + 744)
        HN = at("mlstm_rows", [P, 2, 4 * HD], W_X + 760)
        PSUMS = at("prob_sums", [P, 4], W_X + 1272)
        assert base + 4 * (W_X + 1280) <= nc.sbuf_usable_end

        modrow = at("modulation_rows", [2, DEPTH, 48 * P], p_at(0))
        xnat = at("tokens_natural", [P, NC, D], p_at(16))
        vrow = at("parameter_rows", [P, 2, P], p_at(24))
        wm = at("w_mod_ring", [P, 3, DK, 512], u_at(0))
        mask_in = at("level_masks_in", [P, LEVELS + 1, C], W_LO)
        sqb = at("squares", [P, 2, T], p_at(20))
        rsb = at("inverse_rms", [P, T], p_at(22))
        tb = at("scaled", [P, 2, T], p_at(23))
        wg_raw = at("gate_weights", [P, DK, P], p_at(0))
        wg_hi = at("gate_weights_high", [P, DK, P], p_at(0) + 1024, F32R)
        wg_lo = at("gate_weights_low", [P, DK, P], p_at(0) + 2048, F32R)
        hidh = at("hidden_high", [P, DK, T], p_at(0), F32R)
        hidl = at("hidden_low", [P, DK, T], p_at(8), F32R)
        relu = at("hidden_relu", [P, 2, T], p_at(16))
        hsq = at("hidden_square", [P, 2, T], p_at(18))
        Y = at("conv", [P, 4, T], u_at(0))
        DD = [at("decay_scores_0", [P, 2, 4 * C], u_at(0)), at("decay_scores_1", [P, 2, 4 * C], u_at(8) + 1568)]
        qG0 = at("q_decayed_fwd", [P, 4 * C], u_at(0) + 1024)
        g_b = at("gate_cumsum", [64, T], u_at(2))
        g_e = at("gate_key_decay", [64, T], u_at(3))
        qz = at("q_one_head", [P, 4, T], u_at(4))
        V1 = at("v_and_ones", [P, NC, 4, HD + 1], u_at(8))
        g_lf = at("gate_forget", [P, T], u_at(12))
        g_ig = at("gate_input", [64, T], u_at(13))
        g_m = at("gate_max", [P, T], u_at(14))
        resets = at("chunk_resets", [64, T], u_at(15))
        qG1 = at("q_decayed_bwd", [P, 4 * C], u_at(15))
        kE = at("k_decayed", [P, 2, 4 * HD], u_at(0))
        Cst = [at(f"mlstm_states_{d}", [P, 2, NC, HD + 1], p_at(16 + 4 * d)) for d in range(2)]
        qG = [qG0, qG1]
        Qfb = at("q_decayed", [P, 2, 2 * T], u_at(0))
        Kfb = at("k_decayed_hg", [P, 2, 2 * T], u_at(4))
        Qz = at("q_level", [P, 2, 2 * T], u_at(8))
        Kc = at("k_level", [P, 2 * T], u_at(12))
        A = at("scores", [P, NC, 4, C], p_at(16))
        pyramid = [PT_[:, HZ:HZ + 4, :].rearrange("p t n -> p (t n)"), at("forget_2", [P, 2 * T], u_at(14))]
        word = p_at(20)
        for lv in range(2, LEVELS + 1):
            pyramid.append(at(f"forget_{1 << lv}", [P, 4 * T >> lv], word))
            word += 4 * T >> lv
        Vz = at("v_one_head", [P, NC, 4, P], p_at(HZ))
        Sst = at("hg_states", [P, 2, 2, NC, P], u_at(8))
        kn = at("k_natural", [P, 2, 2, P], u_at(12))
        hsqr = at("hg_squares", [P, 2, T], u_at(0))
        hrs = at("hg_inverse_rms", [P, 2, T], u_at(2))
        hsg = at("hg_silu_gate", [P, 2, T], u_at(4))
        kz = at("k_one_half", [P, 4, T], u_at(0))
        Va = at("attn_v", [P, NC, P], u_at(4))
        PTr = at("probs_transposed", [P, 2, NC, LAT], u_at(6))
        Pb = at("probs", [P, 2, T], u_at(14))
        AO = at("attn_out", [P, 4, T], p_at(8))
        asq = at("attn_squares", [P, 2, T], p_at(12))
        ars = at("attn_inverse_rms", [P, 2, T], p_at(14))
        rt = at("rope_sin_part", [P, 2, LAT], p_at(18))
        onat = at("out_rows", [P, 4, D], p_at(0))

        PS = es.enter_context(nc.psum_tensor("psum", [P, 8, 512], F32))

        sems = {}

        def signal(name, per_layer=0):
            s = Signal(es.enter_context(nc.semaphore(name)), per_layer)
            sems[name] = s
            return s

        const_loaded = signal("const_loaded")
        x_loaded = signal("x_loaded")
        gate_bias_zero = signal("gate_bias_zero")
        wm_loaded = [signal(f"wm_loaded_{r}") for r in range(3)]
        par_T = signal("par_T")
        par_ready = signal("par_ready")
        c_exp = signal("c_exp")
        c_silu = signal("c_silu")
        x_T = signal("x_T")
        x_act = signal("x_act")
        x_dve = signal("x_dve")
        mod_mm = signal("mod_mm")
        mod_row = signal("mod_row")
        mod_T = signal("mod_T")
        mod_ready = signal("mod_ready")
        lb_exp = signal("lb_exp")
        lb_max = signal("lb_max")
        dve_step = signal("dve_step")
        act_step = signal("act_step")
        pool_step = signal("pool_step")

        w_loaded = [signal(f"w_loaded_{r}") for r in range(4)]
        w_high = signal("w_high", 96)
        w_low = signal("w_low", 96)
        gemm = signal("gemm", 96)
        evac_act = signal("evac_act", 56)
        evac_dve = signal("evac_dve", 40)
        u_high = signal("u_high_ready", 24)
        u_ready = signal("u_ready", 24)
        n_square = signal("n_square", 16)
        n_stat = signal("n_stat", 16)
        n_rs = signal("n_rs", 2)
        n_scaled = signal("n_scaled", 16)
        hid_high = signal("hid_high", 32)
        hid_square = signal("hid_square", 32)
        hid_ready = signal("hid_ready", 32)

        wg_loaded = signal("wg_loaded", 64)
        wg_high = signal("wg_high_ready", 1)
        wg_low = signal("wg_low_ready", 1)
        gate_mm = signal("gate_mm", 1)
        gate_tok = signal("gate_tok", 1)

        conv_done = signal("conv_done", 4)
        ml_exp = signal("ml_exp", 4)
        ml_q = signal("ml_q", 2)
        ml_k = signal("ml_k", 2)
        qz_done = signal("qz_done", 4)
        g_softplus = signal("g_softplus", 1)
        g_rows = signal("g_rows", 1)
        g_exp = signal("g_exp", 1)
        v1_ones = signal("v1_ones", 1)
        vT = signal("vT", NC)
        v1_done = signal("v1_done", NC)
        gT = signal("gT", NC)
        gcol_done = signal("gcol_done", NC)
        gc_mm = signal("gc_mm", 1)
        gc_done = signal("gc_done", 1)
        kT = signal("kT", 10)
        kE_done = signal("kE_done", 10)
        kv = signal("kv", 10)
        cst_done = signal("cst_done", 10)
        o_exp = signal("o_exp", 1)
        m_scores = signal("m_scores", 6)
        m_a = signal("m_a", 12)
        m_g = signal("m_g", 12)
        m_arg = signal("m_arg", 12)
        m_qg = signal("m_qg", 12)
        m_dexp = signal("m_dexp", 12)
        m_rows = signal("m_rows", 6)
        m_turned = signal("m_turned", 6)
        m_read = signal("m_read", 12)
        o_clamped = signal("o_clamped", 1)
        z_clamped = signal("z_clamped", 1)
        g_clamped = signal("g_clamped", 1)
        m_ds = signal("m_ds", 12)
        m_num = signal("m_num", 12)
        m_out = signal("m_out", 6)

        z_exp = signal("z_exp", 1)
        h_f = signal("h_f", 1)
        h_copied = signal("h_copied", 8)
        h_scores = signal("h_scores", 8)
        h_masked = signal("h_masked", 8)
        h_updated = signal("h_updated", 7)
        vz_zero = signal("vz_zero", 1)
        sst_zero = signal("sst_zero", 1)
        hvT = signal("hvT", NC)
        vz_done = signal("vz_done", NC)
        hkT = signal("hkT", 10)
        kn_done = signal("kn_done", 10)
        hkv = signal("hkv", 10)
        sst_done = signal("sst_done", 10)
        h_o = signal("h_o", 6)
        h_oe = signal("h_oe", 6)
        h_sq = signal("h_sq", 2)
        h_ms = signal("h_ms", 2)
        h_rs = signal("h_rs", 2)
        g_silu_exp = signal("g_silu_exp", 1)
        hg_done = signal("hg_done", 1)

        a_sq = signal("a_sq", 5)
        a_ms = signal("a_ms", 5)
        a_rs = signal("a_rs", 5)
        a_norm = signal("a_norm", 5)
        a_rot = signal("a_rot", 5)
        a_sin = signal("a_sin", 5)
        a_rope = signal("a_rope", 5)
        kz_mm = signal("kz_mm", 4)
        kz_done = signal("kz_done", 4)
        avT = signal("avT", NC)
        va_done = signal("va_done", NC)
        NU0 = 8 * 6
        a_s = signal("a_s", NU0)
        a_max = signal("a_max", NU0)
        a_exp = signal("a_exp", NU0)
        a_T = signal("a_T", NU0)
        a_Tact = signal("a_Tact", NU0 // 2)
        a_Tdve = signal("a_Tdve", NU0 // 2)
        a_pv = signal("a_pv", 16)
        a_scaled = signal("a_scaled", NU0)
        a_out = signal("a_out", 16)
        out_T = signal("out_T")
        out_act = signal("out_act")
        out_dve = signal("out_dve")
        stored = signal("stored")

        def const(col, n, rows=P):
            return K[0:rows, col:col + n]

        def tok(i):
            return slice(i * C, (i + 1) * C)

        ident = const(K_ID, P)

        def par(col, n=1):
            return V[:, col:col + n]

        def slots(l):
            return 96 * l, 96 * l + 24, 96 * l + 32

        def segs(l):
            return SEGS if l == 0 else SEGS[1:]

        def attn_units(l):
            units, prods = [], []
            for h in range(8):
                if l == 0:
                    units += [(h, q, 2, len(prods)) for q in range(2)]
                    prods.append((h, 0, 2, 2))
                units += [(h, 2 + q, NC, len(prods)) for q in range(4)]
                prods.append((h, 2, 4, NC))
            return units, prods

        def turned_at(l, u):
            return (a_Tdve if u % 2 else a_Tact).at(l, u // 2 + 1)

        block = es.enter_context(nc.Block())

        @block.sync
        def _(sp):
            def load_slot(n, src):
                if not isinstance(n, int) or n >= 4:
                    sp.wait_ge(w_high.sem, n - 3)
                    sp.wait_ge(w_low.sem, n - 3)

            def load(n, j, src):
                load_slot(n, src)
                sp.dma_start(raw[:, j % 4, :, :], src).then_inc(w_loaded[j % 4].sem, 16)

            sp.dma_start(K[:, :], consts).then_inc(const_loaded.sem, 16)
            sp.dma_start(mask_in[:, :, :], level_masks).then_inc(const_loaded.sem, 16)
            sp.dma_start(vrow[0:96, 0, :], b_mod.rearrange("l (r c) -> (l r) c", c=P)).then_inc(const_loaded.sem, 16)
            sp.dma_start(vrow[96:112, 0, :], norm_mix.rearrange("l (r c) -> (l r) c", c=P)).then_inc(const_loaded.sem, 16)
            sp.dma_start(vrow[112:128, 0, :], norm_ffn.rearrange("l (r c) -> (l r) c", c=P)).then_inc(const_loaded.sem, 16)
            for l in range(DEPTH):
                sp.dma_start(vrow[24 * l:24 * l + 24, 1, :],
                             b_in[l, 0:3072].rearrange("(r c) -> r c", c=P)).then_inc(const_loaded.sem, 16)
            sp.dma_start(vrow[48:56, 1, :], hg_lb.rearrange("l d (t c) -> (l d t) c", c=P)).then_inc(const_loaded.sem, 16)
            sp.dma_start(vrow[56:80, 1, :], ml_conv.rearrange("l j (t c) -> (l j t) c", c=P)).then_inc(const_loaded.sem, 16)
            for row, g in ((80, q_norm), (82, k_norm), (84, hg_norm)):
                for half in range(2):
                    sp.dma_start(vrow[row:row + 2, 1, 64 * half:64 * half + 64], g).then_inc(const_loaded.sem, 16)
            sp.dma_start(vrow[86:94, 1, :], c.rearrange("a (r c) -> (a r) c", c=P)).then_inc(const_loaded.sem, 16)
            sp.dma_start(vrow[94:102, 1, :], c_ctx.rearrange("(r c) -> r c", c=P)).then_inc(const_loaded.sem, 16)
            sp.dma_start(xnat[:, 0:2, :], ctx_in.rearrange("a (i p) d -> p (a i) d", p=P)).then_inc(x_loaded.sem, 16)
            sp.dma_start(xnat[:, 2:6, :], x.rearrange("a (i p) d -> p (a i) d", p=P)).then_inc(x_loaded.sem, 16)
            for s in range(24):
                if s >= 3:
                    sp.wait_ge(mod_mm.sem, s - 2)
                sp.dma_start(wm[:, s % 3, :, :],
                             w_mod[s // 12, :, 512 * (s % 12):512 * (s % 12) + 512]
                             .rearrange("(k p) m -> p k m", p=P)).then_inc(wm_loaded[s % 3].sem, 16)
            for l in range(DEPTH):
                n_in, n_out, n_ff = slots(l)
                win = w_in[l, :, 0:3072].rearrange("(k p) (j m) -> j p k m", p=P, m=P)
                for j in range(4):
                    load(n_in + j, j, win[j])
                with sp.Fori(1, 6) as i:
                    for j in range(4):
                        load(n_in + i * 4 + j, j, win[i * 4 + j])
                wout = w_out[l].rearrange("(k p) (j m) -> j p k m", p=P, m=P)
                with sp.Fori(0, 2) as i:
                    for j in range(4):
                        load(n_out + i * 4 + j, j, wout[i * 4 + j])
                w1 = w_ff1[l].rearrange("(k p) (j m) -> j p k m", p=P, m=P)
                w2 = w_ff2[l].rearrange("(g k p) (j m) -> g j p k m", p=P, k=DK, m=P)
                with sp.Fori(0, FG) as g:
                    for j in range(8):
                        load(n_ff + g * 16 + j, j, w1[g * 8 + j])
                    for j in range(8):
                        load(n_ff + g * 16 + 8 + j, j, w2[g, j])
            for i in range(4):
                sp.wait_ge(out_act.sem, i + 1)
                sp.wait_ge(out_dve.sem, i + 1)
                sp.dma_start(out[0, C * i:C * i + C, :], onat[:, i, :]).then_inc(stored.sem, 16)
            sp.wait_ge(stored.sem, 64)

        @block.gpsimd
        def _(pool):
            steps = [0]

            def own(ins):
                steps[0] += 1
                ins.then_inc(pool_step.sem, 1)
                pool.wait_ge(pool_step.sem, steps[0])

            own(pool.memset(GB[:, :], 0.0))
            for l in range(DEPTH):
                for q in range(4):
                    pool.dma_start(GB[32 * q:32 * q + 4, l:l + 1],
                                   b_in[l, 3072 + 4 * q:3076 + 4 * q].rearrange("(a b) -> a b", b=1))\
                        .then_inc(gate_bias_zero.sem, 16)
            pool.wait_ge(mod_ready.sem, 1)
            for l in range(DEPTH):
                if l:
                    pool.wait_ge(*gemm.at(l, 0))
                    pool.wait_ge(*u_ready.at(l, 1))
                own(pool.memset(wg_raw[:, :, :], 0.0))
                for q in range(4):
                    pool.dma_start(wg_raw[:, :, 32 * q:32 * q + 4],
                                   w_in[l, :, 3072 + 4 * q:3076 + 4 * q].rearrange("(k p) m -> p k m", p=P))\
                        .then_inc(wg_loaded.sem, 16)
                pool.wait_ge(*gemm.at(l, 24))
                pool.memset(V1[:, :, :, HD:HD + 1], 1.0).then_inc(v1_ones.sem, 1)
                pool.wait_ge(*evac_act.at(l, 24))
                for clamped, tile, n in ((o_clamped, MO, 2), (z_clamped, HZ, 4)):
                    pool.tensor_scalar(PT_[:, tile:tile + n, :], PT_[:, tile:tile + n, :], -41.0, 0.0, ALU.max, ALU.add)\
                        .then_inc(clamped.sem, 1)
                pool.wait_ge(*h_updated.at(l, 1))
                pool.memset(Vz[:, :, :, :], 0.0).then_inc(vz_zero.sem, 1)
                pool.wait_ge(*h_scores.at(l, 8))
                pool.memset(Sst[:, :, :, :, :], 0.0).then_inc(sst_zero.sem, 1)

        @block.tensor
        def _(pe):
            mm = nc.tensor.matmul
            tr = nc.tensor.transpose

            def gemm_slot(l, n, j, rhs_hi, rhs_lo, free, ss, ready=None):
                pe.wait_ge(w_low.sem, n + 1)
                if free is not None:
                    pe.wait_ge(*free)
                for k in range(DK):
                    if ready is not None:
                        pe.wait_ge(*ready(k))
                    for bank, (t0, tn) in enumerate(SEGS):
                        if (t0, tn) not in ss:
                            continue
                        o = PS[:, 2 * (j % 2) + bank, 0:tn]
                        a, b = whi[:, j % 2, k, :], wlo[:, j % 2, k, :]
                        h, lo = rhs_hi[:, k, t0:t0 + tn], rhs_lo[:, k, t0:t0 + tn]
                        mm(o, b, h, start=(k == 0), stop=False)
                        mm(o, a, lo, start=False, stop=False)
                        last = mm(o, a, h, start=False, stop=(k == DK - 1))
                last.then_inc(gemm.sem, 1)

            def stats(l, w, ss):
                for k in range(DK):
                    pe.wait_ge(*n_square.at(l, 8 * w + k + 1))
                    for bank, (t0, tn) in enumerate(SEGS):
                        if (t0, tn) in ss:
                            last = mm(PS[:, 4 + bank, 0:tn], const(K_ONE, P), sqb[:, k % 2, t0:t0 + tn],
                                      start=(k == 0), stop=(k == DK - 1))
                    last.then_inc(n_stat.sem, 1)

            pe.wait_ge(const_loaded.sem, 17 * 16)
            tr(PS[:, 0, 0:P], vrow[:, 0, :], ident)
            tr(PS[:, 0, P:P + 102], vrow[0:102, 1, :], ident[0:102, 0:102]).then_inc(par_T.sem, 1)
            pe.wait_ge(x_loaded.sem, 32)
            for n in range(12):
                i, half = n // 2, n % 2
                if n >= 4:
                    pe.wait_ge((x_act if n % 2 == 0 else x_dve).sem, (n - 4) // 2 + 1)
                for q in range(4):
                    k = 4 * half + q
                    last = tr(PS[:, 2 + n % 4, q * P:q * P + P], xnat[:, i, k * P:k * P + P], ident)
                last.then_inc(x_T.sem, 1)
            pe.wait_ge(c_silu.sem, 1)
            for s in range(24):
                pe.wait_ge(wm_loaded[s % 3].sem, 16 * (s // 3 + 1))
                if s >= 2:
                    pe.wait_ge(mod_row.sem, s - 1)
                for k in range(DK):
                    last = mm(PS[0:2, 6 + s % 2, :], CS[:, k, :], wm[:, s % 3, k, :], start=(k == 0), stop=(k == DK - 1))
                last.then_inc(mod_mm.sem, 1)
            pe.wait_ge(mod_row.sem, 24)
            for l in range(DEPTH):
                for m in range(48):
                    last = mm(PS[:, 1, 96 * l + 2 * m:96 * l + 2 * m + 2], modrow[0:2, l, m * P:m * P + P],
                              ident[0:2, 0:2], start=True, stop=True)
            last.then_inc(mod_T.sem, 1)

            def mlstm(l):
                i0 = 0 if l == 0 else 2
                for i in range(NC):
                    if i >= 2:
                        pe.wait_ge(*v1_done.at(l, i - 1))
                    if i == 0:
                        pe.wait_ge(*evac_act.at(l, 24))
                    tr(PS[:, i % 2, 0:P], PT_[:, MV, tok(i)], ident)
                    tr(PS[:, i % 2, P:2 * P], PT_[:, MV + 1, tok(i)], ident).then_inc(vT.sem, 1)
                pe.wait_ge(*g_exp.at(l, 1))
                for i in range(NC):
                    if i >= 2:
                        pe.wait_ge(*gcol_done.at(l, i - 1))
                    tr(PS[:, 2 + i % 2, 0:P], PT_[:, GT, tok(i)], ident)
                    tr(PS[:, 2 + i % 2, P:2 * P], g_m[:, tok(i)], ident).then_inc(gT.sem, 1)
                for q in range(4):
                    last = mm(PS[:, 4, NC * q:NC * q + NC], const(K_PAIR + q * P, P, 64), g_lf[0:64, C - 1::C],
                              start=True, stop=True)
                last.then_inc(gc_mm.sem, 1)
                pe.wait_ge(*ml_k.at(l, 2))

                def k_natural(u):
                    s, d = u // 2, u % 2
                    ch = ORDER[d][s]
                    if u >= 2:
                        pe.wait_ge(*kE_done.at(l, u - 1))
                    tr(PS[:, 5 + d, 0:P], PT_[:, MK, tok(ch)], ident)
                    tr(PS[:, 5 + d, P:2 * P], PT_[:, MK + 1, tok(ch)], ident).then_inc(kT.sem, 1)

                def key_value(u):
                    s, d = u // 2, u % 2
                    ch = ORDER[d][s]
                    pe.wait_ge(*kE_done.at(l, u + 1))
                    pe.wait_ge(*v1_done.at(l, NC))
                    if u >= 2:
                        pe.wait_ge(*cst_done.at(l, u - 1))
                    elif d == 1:
                        pe.wait_ge(*gc_done.at(l, 1))
                    bank = 7 if d == 0 else 4
                    for h in range(4):
                        pr = h % 2
                        w0 = (h // 2) * (HD + 1)
                        last = mm(PS[64 * pr:64 * pr + 64, bank, w0:w0 + HD + 1],
                                  kE[:, d, h * HD:h * HD + HD], V1[:, ch, h, :], start=True, stop=True)
                    last.then_inc(kv.sem, 1)

                k_natural(0)
                for u in range(10):
                    if u < 9:
                        k_natural(u + 1)
                    key_value(u)
                pe.wait_ge(*qz_done.at(l, 4))
                pe.wait_ge(*cst_done.at(l, 10))
                pe.wait_ge(*gcol_done.at(l, NC))

                def spread(g, bank, i, d):
                    row = g[0:64, tok(STEP[d][i])]
                    if d:
                        row = row[:, ::-1]
                    for h in range(4):
                        last = mm(PS[:, bank + d, h * C:h * C + C], const(K_SEL + (4 * d + h) * P, P, 64),
                                  row, start=True, stop=True)
                    return last

                def scores(r):
                    i = i0 + r
                    for d in range(2):
                        if r:
                            pe.wait_ge(*m_arg.at(l, 2 * r))
                        spread(g_b, 1, i, d).then_inc(m_a.sem, 1)
                    if r:
                        pe.wait_ge(*m_ds.at(l, 2 * r))
                    for h in range(4):
                        last = mm(PS[:, 0, h * C:h * C + C], PT_[:, MK + h // 2, tok(i)], qz[:, h, tok(i)],
                                  start=True, stop=True)
                    last.then_inc(m_scores.sem, 1)

                scores(0)
                for i in range(i0, NC):
                    r = i - i0
                    for d in range(2):
                        if r:
                            pe.wait_ge(*m_read.at(l, 2 * r))
                        spread(g_lf, 3, i, d).then_inc(m_g.sem, 1)
                    for d in range(2):
                        pe.wait_ge(*m_qg.at(l, 2 * r + d + 1))
                        pe.wait_ge(*m_ds.at(l, 2 * r + d + 1))
                        s = STEP[d][i]
                        for h in range(4):
                            o = PS[:, 3 + d, h * (HD + 1):(h + 1) * (HD + 1)]
                            last = mm(o, DD[r % 2][:, d, h * C:h * C + C], V1[:, i, h, :], start=True, stop=(s == 0))
                            if s:
                                last = mm(o, qG[d][:, h * C:h * C + C], Cst[d][:, h // 2, s, :], start=False, stop=True)
                        last.then_inc(m_num.sem, 1)
                    if i + 1 < NC:
                        scores(r + 1)
                    pe.wait_ge(*m_rows.at(l, r + 1))
                    if r:
                        pe.wait_ge(*m_out.at(l, r))
                    for t in range(2):
                        last = tr(PS[:, 5, t * P:t * P + P], HN[:, 0, t * P:t * P + P], ident)
                    last.then_inc(m_turned.sem, 1)

            def hgrn(l):
                i0 = 0 if l == 0 else 2
                pe.wait_ge(*m_out.at(l, NC - i0))

                def scores(e):
                    pe.wait_ge(*h_copied.at(l, e + 1))
                    if e:
                        pe.wait_ge(*h_masked.at(l, e))
                    for i in range(i0, NC):
                        for h in range(4):
                            t0 = (h // 2) * T + i * C
                            last = mm(PS[:, i, h * C:h * C + C], Kc[:, t0:t0 + C], Qz[:, h % 2, t0:t0 + C],
                                      start=True, stop=True)
                    last.then_inc(h_scores.sem, 1)

                scores(0)
                scores(1)
                for i in range(NC):
                    if i >= 2:
                        pe.wait_ge(*vz_done.at(l, i - 1))
                    tr(PS[:, 6 + i % 2, 0:P], PT_[:, HV, tok(i)], ident)
                    tr(PS[:, 6 + i % 2, P:2 * P], PT_[:, HV + 1, tok(i)], ident).then_inc(hvT.sem, 1)
                for e in range(2, LEVELS + 1):
                    scores(e)
                pe.wait_ge(*h_updated.at(l, 7))
                pe.wait_ge(*h_masked.at(l, 8))
                pe.wait_ge(*vz_done.at(l, NC))

                def k_natural(u):
                    s, d = u // 2, u % 2
                    if u >= 2:
                        pe.wait_ge(*kn_done.at(l, u - 1))
                    t0 = ORDER[d][s] * C
                    tr(PS[:, d, 0:P], Kfb[:, d, t0:t0 + C], ident)
                    tr(PS[:, d, P:2 * P], Kfb[:, d, T + t0:T + t0 + C], ident).then_inc(hkT.sem, 1)

                def key_value(u):
                    s, d = u // 2, u % 2
                    pe.wait_ge(*kn_done.at(l, u + 1))
                    if u >= 2:
                        pe.wait_ge(*sst_done.at(l, u - 1))
                    for h in range(4):
                        pr = h % 2
                        last = mm(PS[:, 2 + d, h * HD:h * HD + HD], kn[:, d, h // 2, :],
                                  Vz[:, ORDER[d][s], h, 64 * pr:64 * pr + 64], start=True, stop=True)
                    last.then_inc(hkv.sem, 1)

                k_natural(0)
                for u in range(10):
                    if u < 9:
                        k_natural(u + 1)
                    key_value(u)
                pe.wait_ge(*sst_done.at(l, 10))
                for i in range(i0, NC):
                    for t in range(2):
                        o = PS[:, (4 + i) % 8, t * P:t * P + P]
                        first = True
                        for d in range(2):
                            s = STEP[d][i]
                            if s:
                                mm(o, Sst[:, d, t, s, :], Qfb[:, d, t * T + i * C:t * T + i * C + C], start=first,
                                   stop=False)
                                first = False
                        mm(o, Vz[:, i, 2 * t, :], A[:, i, 2 * t, :], start=first, stop=False)
                        last = mm(o, Vz[:, i, 2 * t + 1, :], A[:, i, 2 * t + 1, :], start=False, stop=True)
                    last.then_inc(h_o.sem, 1)
                for t in range(2):
                    pe.wait_ge(*h_sq.at(l, t + 1))
                    for bank, (t0, tn) in enumerate(SEGS):
                        if l == 0 or bank:
                            last = mm(PS[:, 2 * t + bank, 0:tn], const(K_BLK, P), hsqr[:, t, t0:t0 + tn],
                                      start=True, stop=True)
                    last.then_inc(h_ms.sem, 1)

            def attention(l):
                pe.wait_ge(*hg_done.at(l, 1))
                for j in range(5):
                    if j >= 2:
                        pe.wait_ge(*a_rs.at(l, j - 1))
                    pe.wait_ge(*a_sq.at(l, j + 1))
                    for bank, (t0, tn) in enumerate(SEGS):
                        last = mm(PS[:, 2 * (j % 2) + bank, 0:tn], const(K_BLK, P), asq[:, j % 2, t0:t0 + tn],
                                  start=True, stop=True)
                    last.then_inc(a_ms.sem, 1)
                for j in range(5):
                    pe.wait_ge(*a_norm.at(l, j + 1))
                    if j >= 2:
                        pe.wait_ge(*a_sin.at(l, j - 1))
                    mm(PS[:, 4 + j % 2, :], const(K_ROT, P), PT_[:, AQ + j, CTX:T], start=True, stop=True)\
                        .then_inc(a_rot.sem, 1)
                for i in range(NC):
                    if i >= 2:
                        pe.wait_ge(*va_done.at(l, i - 1))
                    tr(PS[:, 6 + i % 2, 0:P], PT_[:, AV, tok(i)], ident).then_inc(avT.sem, 1)
                pe.wait_ge(*a_rope.at(l, 5))
                for q in range(4):
                    if q >= 2:
                        pe.wait_ge(*kz_done.at(l, q - 1))
                    elif q == 0:
                        pe.wait_ge(*a_rs.at(l, 5))
                    for bank, (t0, tn) in enumerate(SEGS):
                        last = mm(PS[:, 2 * (q % 2) + bank, 0:tn], const(K_KZ + q * P, P), PT_[:, AK, t0:t0 + tn],
                                  start=True, stop=True)
                    last.then_inc(kz_mm.sem, 1)
                pe.wait_ge(*kz_done.at(l, 4))
                units, prods = attn_units(l)

                def score(u):
                    h, q, nk, _ = units[u]
                    if u >= 2:
                        pe.wait_ge(*a_exp.at(l, u - 1))
                    lhs = PT_[:, AQ + h // 2, tok(q)]
                    kk = kz[:, 2 * (h // 4) + h % 2, :]
                    last = mm(PS[:, 2 * (u % 2), 0:min(nk, 4) * C], lhs, kk[:, 0:min(nk, 4) * C], start=True, stop=True)
                    if nk > 4:
                        last = mm(PS[:, 2 * (u % 2) + 1, 0:(nk - 4) * C], lhs, kk[:, 4 * C:nk * C], start=True, stop=True)
                    last.then_inc(a_s.sem, 1)

                def turn(u):
                    h, q, nk, pr = units[u]
                    pe.wait_ge(*a_scaled.at(l, u + 1))
                    if u:
                        pe.wait_ge(*turned_at(l, u - 1))
                    else:
                        pe.wait_ge(*a_sin.at(l, 5))
                    for kt in range(nk):
                        last = tr(PS[:, 4 + kt // 4, (kt % 4) * P:(kt % 4) * P + P], Pb[:, u % 2, tok(kt)], ident)
                    last.then_inc(a_T.sem, 1)

                def product(u):
                    h, q, nk, pr = units[u]
                    h, q0, nq, nk = prods[pr]
                    if q != q0 + nq - 1:
                        return
                    pe.wait_ge(*turned_at(l, u))
                    if u:
                        pe.wait_ge(*turned_at(l, u - 1))
                    pe.wait_ge(*va_done.at(l, NC))
                    if pr >= 2:
                        pe.wait_ge(*a_out.at(l, pr - 1))
                    r0, g0 = 64 * (h % 2), 64 * (h // 4)
                    for kt in range(nk):
                        last = mm(PS[r0:r0 + 64, 6 + pr % 2, 0:nq * C], Va[:, kt, g0:g0 + 64], PTr[:, pr % 2, kt, 0:nq * C],
                                  start=(kt == 0), stop=(kt == nk - 1))
                    last.then_inc(a_pv.sem, 1)

                score(0)
                for u in range(len(units)):
                    if u + 1 < len(units):
                        score(u + 1)
                    turn(u)
                    if u:
                        product(u - 1)
                product(len(units) - 1)

            for l in range(DEPTH):
                n_in, n_out, n_ff = slots(l)
                stats(l, 0, SEGS)
                pe.wait_ge(*wg_low.at(l, 1))
                for k in range(DK):
                    pe.wait_ge(*u_ready.at(l, k + 1))
                    for bank, (t0, tn) in enumerate(SEGS):
                        o = PS[:, 6 + bank, 0:tn]
                        mm(o, wg_lo[:, k, :], Uh[:, k, t0:t0 + tn], start=(k == 0), stop=False)
                        mm(o, wg_hi[:, k, :], Ul[:, k, t0:t0 + tn], start=False, stop=False)
                        last = mm(o, wg_hi[:, k, :], Uh[:, k, t0:t0 + tn], start=False, stop=(k == DK - 1))
                last.then_inc(gate_mm.sem, 1)
                for j in range(4):
                    free = evac_act.at(l, j - 1) if j >= 2 else (evac_dve.at(l, 0) if l else None)
                    gemm_slot(l, n_in + j, j, Uh, Ul, free, SEGS)
                with pe.Fori(1, 6) as i:
                    for j in range(4):
                        gemm_slot(l, n_in + i * 4 + j, j, Uh, Ul, (evac_act.sem, 56 * l + i * 4 + j - 1), SEGS)
                mlstm(l)
                hgrn(l)
                attention(l)
                pe.wait_ge(*a_out.at(l, len(attn_units(l)[1])))
                for j in range(8):
                    gemm_slot(l, n_out + j, j, Uh, Ul, evac_dve.at(l, j - 1) if j >= 2 else None, segs(l),
                              (lambda k: u_ready.at(l, 9 + k)) if j == 0 else None)
                stats(l, 1, segs(l))

                def mlp(g, n0):
                    for j in range(8):
                        free = (evac_dve.sem, 40 * l + g * 8 + 7 + j) if j < 2 else \
                            (evac_act.sem, 56 * l + 24 + g * 8 + j - 1)
                        pe.wait_ge(u_ready.sem, 24 * l + 24)
                        gemm_slot(l, n_ff + g * 16 + j, j, Uh, Ul, free, segs(l))
                    for j in range(8):
                        free = (evac_act.sem, 56 * l + 24 + g * 8 + 7 + j) if j < 2 else \
                            (evac_dve.sem, 40 * l + 8 + g * 8 + j - 1)
                        gemm_slot(l, n_ff + g * 16 + 8 + j, j, hidh, hidl, free, segs(l),
                                  (lambda k: (hid_ready.sem, 32 * l + g * 8 + k + 1)) if j == 0 else None)

                with pe.Fori(0, FG) as g:
                    mlp(g, n_ff)
            for i in range(4):
                if i >= 2:
                    pe.wait_ge(out_act.sem, i - 1)
                    pe.wait_ge(out_dve.sem, i - 1)
                pe.wait_ge(*evac_dve.at(2, 0))
                for half in range(2):
                    for q in range(4):
                        last = tr(PS[:, 4 + 2 * (i % 2) + half, q * P:q * P + P], H[:, 4 * half + q, CTX + i * C:CTX + i * C + C],
                                  ident)
                    last.then_inc(out_T.sem, 1)

        @block.scalar
        def _(act):
            steps = [0]
            ac = nc.scalar.activation

            def own(ins):
                steps[0] += 1
                ins.then_inc(act_step.sem, 1)
                act.wait_ge(act_step.sem, steps[0])

            def split(n, j, wait_value):
                act.wait_ge(w_loaded[j % 4].sem, wait_value)
                act.wait_ge(gemm.sem, n - 1)
                ac(whi[:, j % 2, :, :], raw[:, j % 4, :, :], ACT.Copy).then_inc(w_high.sem, 1)

            def squares(l, w, ss, ready):
                for k in range(DK):
                    if ready is not None:
                        act.wait_ge(*ready(k))
                    if k >= 2:
                        act.wait_ge(*n_stat.at(l, 8 * w + k - 1))
                    t0 = ss[0][0]
                    ac(sqb[:, k % 2, t0:T], H[:, k, t0:T], ACT.Square).then_inc(n_square.sem, 1)
                act.wait_ge(*n_stat.at(l, 8 * w + 8))
                for bank, (t0, tn) in enumerate(SEGS):
                    if (t0, tn) in ss:
                        last = ac(rsb[:, t0:t0 + tn], PS[:, 4 + bank, 0:tn], ACT.Ln, bias=EPST[:, 0:1])
                own(last)
                ac(rsb[:, ss[0][0]:T], rsb[:, ss[0][0]:T], ACT.Exp, scale=-0.5).then_inc(n_rs.sem, 1)

            def u_high_part(l, w, ss):
                shift = 0 if w == 0 else 24
                for k in range(DK):
                    act.wait_ge(*n_scaled.at(l, 8 * w + k + 1))
                    for t0, tn in ss:
                        who = 1 if t0 == 0 else 0
                        last = ac(Uh[:, k, t0:t0 + tn], tb[:, k % 2, t0:t0 + tn], ACT.Identity,
                                  bias=MOD[:, l, shift + k, who:who + 1])
                    last.then_inc(u_high.sem, 1)

            nc.scalar.preload_act_table_set("natural_log_exp_and_others")

            def sigmoid(ap):
                own(ac(ap, ap, ACT.Exp, scale=-1.0))
                own(ac(ap, ap, ACT.Ln, bias=1.0))
                return ac(ap, ap, ACT.Exp, scale=-1.0)

            act.wait_ge(par_ready.sem, 1)
            ac(CS[:, :, :], V[:, V_C:V_C + 16].rearrange("p (w k) -> p k w", w=2), ACT.Exp, scale=-1.0)\
                .then_inc(c_exp.sem, 1)
            act.wait_ge(lb_max.sem, 1)
            ac(LBT[:, 1:3, :], LBT[:, 1:3, :], ACT.Exp).then_inc(lb_exp.sem, 1)
            for n in range(0, 12, 2):
                act.wait_ge(x_T.sem, n + 1)
                i, half = n // 2, n % 2
                ac(H[:, 4 * half:4 * half + 4, tok(i)], PS[:, 2 + n % 4, :].rearrange("p (k c) -> p k c", k=4),
                   ACT.Copy).then_inc(x_act.sem, 1)
            for s in range(24):
                act.wait_ge(mod_mm.sem, s + 1)
                ac(modrow[0:2, s // 12, 512 * (s % 12):512 * (s % 12) + 512], PS[0:2, 6 + s % 2, :], ACT.Copy)\
                    .then_inc(mod_row.sem, 1)

            def mlstm(l):
                i0 = 0 if l == 0 else 2
                own(ac(g_lf[64:P, :], PT_[64:P, GT, :], ACT.Abs))
                own(ac(g_lf[64:P, :], g_lf[64:P, :], ACT.Exp, scale=-1.0))
                ac(g_lf[64:P, :], g_lf[64:P, :], ACT.Ln, bias=1.0).then_inc(g_softplus.sem, 1)
                for i in range(NC):
                    act.wait_ge(*vT.at(l, i + 1))
                    if i == 0:
                        act.wait_ge(*v1_ones.at(l, 1))
                    ac(V1[:, i, :, 0:HD], PS[:, i % 2, 0:256].rearrange("p (h e) -> p h e", h=4), ACT.Copy)\
                        .then_inc(v1_done.sem, 1)
                for j in range(4):
                    act.wait_ge(*conv_done.at(l, j + 1))
                    sigmoid(PT_[:, MQ + j, :]).then_inc(ml_exp.sem, 1)
                for j in range(2):
                    act.wait_ge(*ml_q.at(l, j + 1))
                    for pr in range(2):
                        ac(qz[:, 2 * j + pr, :], Y[:, j, :], ACT.Copy, scale=const(K_HM + pr, 1))\
                            .then_inc(qz_done.sem, 1)
                act.wait_ge(*g_rows.at(l, 1))
                ac(g_lf[0:64, :], g_lf[0:64, :], ACT.Exp)
                ac(PT_[0:32, GT, :], g_ig[0:32, :], ACT.Copy)
                ac(PT_[64:96, GT, :], g_e[0:32, :], ACT.Exp)
                ac(g_m[64:96, :], g_m[0:32, :], ACT.Exp)
                for t0, tn in SEGS:
                    ac(PT_[32:64, GT, t0:t0 + tn], g_ig[32:64, t0:t0 + tn][:, ::-1], ACT.Copy)
                    ac(g_m[96:P, t0:t0 + tn], g_m[32:64, t0:t0 + tn][:, ::-1], ACT.Exp)
                    last = ac(PT_[96:P, GT, t0:t0 + tn], g_e[32:64, t0:t0 + tn][:, ::-1], ACT.Exp)
                last.then_inc(g_exp.sem, 1)
                for i in range(NC):
                    act.wait_ge(*gT.at(l, i + 1))
                    src = PS[:, 2 + i % 2, 0:2 * P].rearrange("p (n d c) -> p n d c", n=4, d=2)
                    ac(GCOL[:, i, 0:2, :, :], src[:, 0:2, :, 0:4], ACT.Copy)
                    ac(GCOL[:, i, 2, :, :], src[:, 3, :, 0:4], ACT.Copy).then_inc(gcol_done.sem, 1)
                act.wait_ge(*o_clamped.at(l, 1))
                sigmoid(PT_[:, MO:MO + 2, :]).then_inc(o_exp.sem, 1)
                for r in range(NC - i0):
                    for d in range(2):
                        act.wait_ge(*m_arg.at(l, 2 * r + d + 1))
                        ac(DD[r % 2][:, d, :], DD[r % 2][:, d, :], ACT.Exp).then_inc(m_dexp.sem, 1)
                    if r == 1:
                        act.wait_ge(*z_clamped.at(l, 1))
                        sigmoid(PT_[:, HZ:HZ + 4, :]).then_inc(z_exp.sem, 1)

            def hgrn(l):
                i0 = 0 if l == 0 else 2
                act.wait_ge(*h_f.at(l, 1))
                for pr in range(2):
                    last = ac(Qz[:, pr, :], PT_[:, HQ:HQ + 2, :].rearrange("p t n -> p (t n)"), ACT.Copy,
                              scale=const(K_HM + pr, 1))
                last.then_inc(h_copied.sem, 1)

                def values():
                    act.wait_ge(*vz_zero.at(l, 1))
                    for i in range(NC):
                        act.wait_ge(*hvT.at(l, i + 1))
                        src = PS[:, 6 + i % 2, 0:256].rearrange("p (h e) -> p h e", h=4)
                        for pr in range(2):
                            last = ac(Vz[:, i, pr::2, 64 * pr:64 * pr + 64], src[:, pr::2, :], ACT.Copy)
                        last.then_inc(vz_done.sem, 1)

                for lv in range(LEVELS):
                    if lv == 2:
                        values()
                    b = 1 << lv

                    def halves(ap):
                        return ap.rearrange("p (n two b) -> p n two b", two=2, b=b)

                    if lv:
                        act.wait_ge(*h_updated.at(l, lv))
                    act.wait_ge(*h_scores.at(l, lv + 1))
                    for pr in range(2):
                        for side, d in ((1, 0), (0, 1)):
                            ac(halves(Qz[:, pr, :])[:, :, side, :], halves(Qfb[:, d, :])[:, :, side, :], ACT.Copy,
                               scale=const(K_HM + pr, 1))
                    ac(halves(Kc[:, :])[:, :, 0, :], halves(Kfb[:, 0, :])[:, :, 0, :], ACT.Copy)
                    ac(halves(Kc[:, :])[:, :, 1, :], halves(Kfb[:, 1, :])[:, :, 1, :], ACT.Copy)\
                        .then_inc(h_copied.sem, 1)
                act.wait_ge(*h_scores.at(l, 8))
                for u in range(10):
                    act.wait_ge(*hkT.at(l, u + 1))
                    if u >= 2:
                        act.wait_ge(*hkv.at(l, u - 1))
                    ac(kn[:, u % 2, :, :], PS[:, u % 2, 0:256].rearrange("p (t c) -> p t c", t=2), ACT.Copy)\
                        .then_inc(kn_done.sem, 1)
                for i in range(i0, NC):
                    act.wait_ge(*h_o.at(l, i - i0 + 1))
                    last = ac(PT_[:, HQ:HQ + 2, tok(i)],
                              PS[:, (4 + i) % 8, 0:256].rearrange("p (t c) -> p t c", t=2),
                              ACT.Copy)
                    last.then_inc(h_oe.sem, 1)
                act.wait_ge(*h_oe.at(l, NC - i0))
                t0 = i0 * C
                for t in range(2):
                    ac(hsqr[:, t, t0:T], PT_[:, HQ + t, t0:T], ACT.Square).then_inc(h_sq.sem, 1)
                act.wait_ge(*g_clamped.at(l, 1))
                sigmoid(hsg[:, :, :]).then_inc(g_silu_exp.sem, 1)
                for t in range(2):
                    act.wait_ge(*h_ms.at(l, t + 1))
                    for bank, (a0, an) in enumerate(SEGS):
                        if a0 >= t0:
                            last = ac(hrs[:, t, a0:a0 + an], PS[:, 2 * t + bank, 0:an], ACT.Ln, bias=EPST[:, 0:1])
                    own(last)
                    ac(hrs[:, t, t0:T], hrs[:, t, t0:T], ACT.Exp, scale=-0.5).then_inc(h_rs.sem, 1)

            def attention(l):
                act.wait_ge(*hg_done.at(l, 1))

                def square(j):
                    if j >= 2:
                        act.wait_ge(*a_ms.at(l, j - 1))
                    ac(asq[:, j % 2, :], PT_[:, AQ + j, :], ACT.Square).then_inc(a_sq.sem, 1)

                square(0)
                for j in range(5):
                    if j < 4:
                        square(j + 1)
                    act.wait_ge(*a_ms.at(l, j + 1))
                    if j >= 2:
                        act.wait_ge(*a_norm.at(l, j - 1))
                    for bank, (t0, tn) in enumerate(SEGS):
                        last = ac(ars[:, j % 2, t0:t0 + tn], PS[:, 2 * (j % 2) + bank, 0:tn], ACT.Ln,
                                  bias=EPST[:, 0:1])
                    own(last)
                    ac(ars[:, j % 2, :], ars[:, j % 2, :], ACT.Exp, scale=-0.5).then_inc(a_rs.sem, 1)
                for i in range(NC):
                    act.wait_ge(*avT.at(l, i + 1))
                    ac(Va[:, i, :], PS[:, 6 + i % 2, 0:P], ACT.Copy)\
                        .then_inc(va_done.sem, 1)
                for q in range(4):
                    act.wait_ge(*kz_mm.at(l, q + 1))
                    for bank, (t0, tn) in enumerate(SEGS):
                        last = ac(kz[:, q, t0:t0 + tn], PS[:, 2 * (q % 2) + bank, 0:tn], ACT.Copy)
                    last.then_inc(kz_done.sem, 1)
                units, prods = attn_units(l)

                def probs(u):
                    h, q, nk, _ = units[u]
                    act.wait_ge(*a_max.at(l, u + 1))
                    if u >= 2:
                        act.wait_ge(*a_T.at(l, u - 1))
                    src = PS[:, 2 * (u % 2):2 * (u % 2) + 2, :].rearrange("p b n -> p (b n)")[:, 0:nk * C]
                    ac(Pb[:, u % 2, 0:nk * C], src, ACT.Exp, bias=NEGM[:, u % 2:u % 2 + 1],
                       accum_out=PSUMS[:, u % 2:u % 2 + 1]).then_inc(a_exp.sem, 1)

                def turned(u):
                    h, q, nk, pr = units[u]
                    q0 = prods[pr][1]
                    if u % 2:
                        return
                    act.wait_ge(*a_T.at(l, u + 1))
                    if pr >= 2:
                        act.wait_ge(*a_pv.at(l, pr - 1))
                    src = PS[:, 4:6, :].rearrange("p b n -> p (b n)")[:, 0:nk * C]
                    ac(PTr[:, pr % 2, 0:nk, (q - q0) * C:(q - q0) * C + C],
                       src.rearrange("p (k c) -> p k c", k=nk), ACT.Copy).then_inc(a_Tact.sem, 1)

                def take(u):
                    h, q, nk, pr = units[u]
                    _, q0, nq, _ = prods[pr]
                    if q != q0 + nq - 1:
                        return
                    act.wait_ge(*a_pv.at(l, pr + 1))
                    r0 = 64 * (h % 2)
                    ac(AO[r0:r0 + 64, h // 2, q0 * C:(q0 + nq) * C], PS[r0:r0 + 64, 6 + pr % 2, 0:nq * C], ACT.Copy)\
                        .then_inc(a_out.sem, 1)

                probs(0)
                for u in range(len(units)):
                    if u + 1 < len(units):
                        probs(u + 1)
                    turned(u)
                    if u >= 2:
                        take(u - 2)
                take(len(units) - 2)
                take(len(units) - 1)

            act.wait_ge(mod_ready.sem, 1)
            for l in range(DEPTH):
                n_in, n_out, n_ff = slots(l)
                act.wait_ge(x_dve.sem, 6)
                act.wait_ge(x_act.sem, 6)
                if l == 0:
                    act.wait_ge(w_loaded[0].sem, 16)
                    ac(whi[:, 0, :, :], raw[:, 0, :, :], ACT.Copy).then_inc(w_high.sem, 1)
                act.wait_ge(*wg_loaded.at(l, 64)) if l == 0 else None
                if l == 0:
                    ac(wg_hi[:, :, :], wg_raw[:, :, :], ACT.Copy).then_inc(wg_high.sem, 1)
                squares(l, 0, SEGS, None if l == 0 else (lambda k: evac_dve.at(l - 1, 8 + 24 + k + 1)))
                u_high_part(l, 0, SEGS)
                if l:
                    act.wait_ge(*wg_loaded.at(l, 64))
                    ac(wg_hi[:, :, :], wg_raw[:, :, :], ACT.Copy).then_inc(wg_high.sem, 1)
                act.wait_ge(*gate_mm.at(l, 1))
                act.wait_ge(gate_bias_zero.sem, 128)
                act.wait_ge(*u_ready.at(l, 8))
                for bank, (t0, tn) in enumerate(SEGS):
                    last = ac(PT_[:, GT, t0:t0 + tn], PS[:, 6 + bank, 0:tn], ACT.Identity, bias=GB[:, l:l + 1])
                last.then_inc(gate_tok.sem, 1)

                def project(i):
                    for j in range(4):
                        n = n_in + i * 4 + j
                        split(n + 1, j + 1, (n_in // 4 + i + 1 + (j + 1) // 4) * 16)
                        act.wait_ge(gemm.sem, n + 1)
                        m = i * 4 + j
                        for bank, (t0, tn) in enumerate(SEGS):
                            last = ac(PT_[:, bass.ts(m, 1), t0:t0 + tn].squeeze(1), PS[:, 2 * (j % 2) + bank, 0:tn],
                                      ACT.Identity, bias=V[:, bass.ts(V_BIN + 24 * l + m, 1)])
                        last.then_inc(evac_act.sem, 1)

                project(0)
                with act.Fori(1, 6) as i:
                    project(i)
                act.wait_ge(*evac_act.at(l, 24))
                act.wait_ge(*gate_tok.at(l, 1))
                mlstm(l)
                hgrn(l)
                attention(l)
                s0 = segs(l)[0][0]
                act.wait_ge(*a_out.at(l, len(attn_units(l)[1])))
                for k in range(DK):
                    src = AO[:, k, s0:T] if k < 4 else PT_[:, (HQ if k < 6 else MO) + k % 2, s0:T]
                    ac(Uh[:, k, s0:T], src, ACT.Copy).then_inc(u_high.sem, 1)
                for j in range(8):
                    n = n_out + j
                    split(n + 1, j + 1, (n + 1) // 4 * 16 + 16)
                squares(l, 1, segs(l), lambda k: evac_dve.at(l, k + 1))
                u_high_part(l, 1, segs(l))

                def mlp(g, last_group=False):
                    for j in range(8):
                        n = n_ff + g * 16 + j
                        split(n + 1, j + 1, (n_ff // 4 + g * 4 + (j + 1) // 4 + 1) * 16)
                        act.wait_ge(gemm.sem, n + 1)
                        f = 32 * l + g * 8 + j
                        if not isinstance(f, int) or f >= 2:
                            act.wait_ge(hid_ready.sem, f - 1)
                        for bank, (t0, tn) in enumerate(SEGS):
                            if (t0, tn) in segs(l):
                                last = ac(relu[:, j % 2, t0:t0 + tn], PS[:, 2 * (j % 2) + bank, 0:tn], ACT.Relu)
                        last.then_inc(evac_act.sem, 1)
                        act.wait_ge(evac_act.sem, 56 * l + 24 + g * 8 + j + 1)
                        t0 = segs(l)[0][0]
                        ac(hidh[:, j, t0:T], relu[:, j % 2, t0:T], ACT.Square).then_inc(hid_high.sem, 1)
                    for j in range(8):
                        n = n_ff + g * 16 + 8 + j
                        if not (last_group and j == 7):
                            split(n + 1, j + 1, (n_ff // 4 + g * 4 + 2 + (j + 1) // 4 + 1) * 16)

                mlp(0)
                if l == 0:
                    with act.Fori(1, FG) as g:
                        mlp(g)
                else:
                    with act.Fori(1, FG - 1) as g:
                        mlp(g)
                    mlp(FG - 1, True)
            for i in range(4):
                act.wait_ge(out_T.sem, 2 * i + 1)
                ac(onat[:, i, 0:512], PS[:, 4 + 2 * (i % 2), :], ACT.Copy).then_inc(out_act.sem, 1)

        @block.vector
        def _(dve):
            steps = [0]
            tt, ts, stt, cp = nc.vector.tensor_tensor, nc.vector.tensor_scalar, nc.vector.scalar_tensor_tensor, \
                nc.vector.tensor_copy

            def own(ins):
                steps[0] += 1
                ins.then_inc(dve_step.sem, 1)
                dve.wait_ge(dve_step.sem, steps[0])

            def low(n, j):
                dve.wait_ge(w_high.sem, n + 1)
                tt(wlo[:, j % 2, :, :], raw[:, j % 4, :, :], whi[:, j % 2, :, :].bitcast(F32), ALU.subtract)\
                    .then_inc(w_low.sem, 1)

            def u_parts(l, w, ss):
                dve.wait_ge(*n_rs.at(l, w + 1))
                shift = 0 if w == 0 else 24
                for k in range(DK + 1):
                    if k < DK:
                        if k >= 2:
                            dve.wait_ge(*u_high.at(l, 16 * w + k - 1))
                            dve.wait_ge(*u_ready.at(l, 16 * w + k - 1))
                        for t0, tn in ss:
                            who = 1 if t0 == 0 else 0
                            last = stt(tb[:, k % 2, t0:t0 + tn], H[:, k, t0:t0 + tn], GAIN[:, l, w, k, who:who + 1],
                                       rsb[:, t0:t0 + tn], ALU.mult, ALU.mult)
                        last.then_inc(n_scaled.sem, 1)
                    if k:
                        dve.wait_ge(*u_high.at(l, 16 * w + k))
                        dve.wait_ge(*n_scaled.at(l, 8 * w + k))
                        for t0, tn in ss:
                            who = 1 if t0 == 0 else 0
                            last = stt(Ul[:, k - 1, t0:t0 + tn], tb[:, (k - 1) % 2, t0:t0 + tn],
                                       MOD[:, l, shift + k - 1, who:who + 1], Uh[:, k - 1, t0:t0 + tn].bitcast(F32),
                                       ALU.add, ALU.subtract)
                        last.then_inc(u_ready.sem, 1)

            dve.wait_ge(par_T.sem, 1)
            dve.wait_ge(const_loaded.sem, 17 * 16)
            own(cp(M8[:, :, :], mask_in[:, :, :]))
            dve.memset(EPST[:, :], EPS)
            cp(V[:, :], PS[:, 0, 0:V_N]).then_inc(par_ready.sem, 1)
            dve.wait_ge(par_ready.sem, 1)
            a0, a1 = V[:, V_LB:V_LB + 4], V[:, V_LB + 4:V_LB + 8]
            own(tt(LBT[:, 0, :], a0, a1, ALU.max))
            tt(LBT[:, 1, :], a0, LBT[:, 0, :], ALU.subtract)
            tt(LBT[:, 2, :], a1, LBT[:, 0, :], ALU.subtract).then_inc(lb_max.sem, 1)
            dve.wait_ge(c_exp.sem, 1)
            own(ts(CS[:, :, :], CS[:, :, :], 1.0, None, ALU.add))
            own(nc.vector.reciprocal(CS[:, :, :], CS[:, :, :]))
            tt(CS[:, :, :], CS[:, :, :], V[:, V_C:V_C + 16].rearrange("p (w k) -> p k w", w=2), ALU.mult)\
                .then_inc(c_silu.sem, 1)
            dve.wait_ge(lb_exp.sem, 1)
            own(tt(LBT[:, 3, :], LBT[:, 1, :], LBT[:, 2, :], ALU.add))
            own(nc.vector.reciprocal(LBT[:, 4, :], LBT[:, 3, :]))
            dve.memset(LB[:, 0, :], 0.0)
            dve.memset(LB1[:, 0, :], 1.0)
            own(tt(LB[:, 1, :], LBT[:, 2, :], LBT[:, 4, :], ALU.mult))
            own(ts(LB1[:, 1, :], LB[:, 1, :], -1.0, 1.0, ALU.mult, ALU.add))
            own(ts(V[:, V_QN:V_QN + 2], V[:, V_QN:V_QN + 2], HD ** -0.5, None, ALU.mult))
            for n in range(1, 12, 2):
                dve.wait_ge(x_T.sem, n + 1)
                i, half = n // 2, n % 2
                cp(H[:, 4 * half:4 * half + 4, tok(i)], PS[:, 2 + n % 4, :].rearrange("p (k c) -> p k c", k=4))\
                    .then_inc(x_dve.sem, 1)
            dve.wait_ge(mod_T.sem, 1)
            for l in range(DEPTH):
                own(tt(MOD[:, l, :, :], PS[:, 1, 96 * l:96 * l + 96].rearrange("p (m w) -> p m w", w=2),
                       V[:, V_BMOD + 48 * l:V_BMOD + 48 * l + 48].unsqueeze(2).broadcast_to([P, 48, 2]), ALU.add))
                for w, (row, g) in enumerate(((8, V_NMIX), (32, V_NFFN))):
                    own(stt(GAIN[:, l, w, :, :], MOD[:, l, row:row + 8, :], 1.0,
                            V[:, g + 8 * l:g + 8 * l + 8].unsqueeze(2).broadcast_to([P, DK, 2]), ALU.add, ALU.mult))
            dve.memset(EPST[:, 1:2], 0.0).then_inc(mod_ready.sem, 1)

            def mlstm(l):
                i0 = 0 if l == 0 else 2
                dve.wait_ge(*evac_act.at(l, 24))

                def tap(w, j):
                    return par(V_CONV + 12 * l + 4 * w + j)

                for j in range(4):
                    last = ts(Y[:, j, :], PT_[:, MQ + j, :], tap(1, j), None, ALU.mult)
                own(last)
                for j in range(4):
                    for a, n in SEGS:
                        last = stt(Y[:, j, a + 1:a + n], PT_[:, MQ + j, a:a + n - 1], tap(0, j), Y[:, j, a + 1:a + n],
                                   ALU.mult, ALU.add)
                own(last)
                for j in range(4):
                    for a, n in SEGS:
                        last = stt(Y[:, j, a:a + n - 1], PT_[:, MQ + j, a + 1:a + n], tap(2, j), Y[:, j, a:a + n - 1],
                                   ALU.mult, ALU.add)
                own(last)
                for j in range(4):
                    ts(PT_[:, MQ + j, :], Y[:, j, :], -41.0, None, ALU.max).then_inc(conv_done.sem, 1)
                dve.wait_ge(*g_softplus.at(l, 1))
                own(stt(g_lf[64:P, :], PT_[64:P, GT, :], 0.0, g_lf[64:P, :], ALU.min, ALU.subtract))
                cp(g_lf[0:32, :], g_lf[64:96, :])
                cp(g_ig[0:32, :], PT_[0:32, GT, :])
                for a, n in SEGS:
                    cp(g_lf[32:64, a:a + n], g_lf[96:128, a:a + n][:, ::-1])
                    cp(g_ig[32:64, a:a + n], PT_[32:64, GT, a:a + n][:, ::-1])
                own(dve.memset(resets[:, :], 1.0))
                own(dve.memset(resets[:, 0:T:C], 0.0))
                for j in range(2):
                    dve.wait_ge(*ml_exp.at(l, j + 1))
                    tt(Y[:, j, :], Y[:, j, :], PT_[:, MQ + j, :], ALU.mult).then_inc(ml_q.sem, 1)
                for j in range(2, 4):
                    dve.wait_ge(*ml_exp.at(l, j + 1))
                    stt(PT_[:, MQ + j, :], Y[:, j, :], HD ** -0.5, PT_[:, MQ + j, :], ALU.mult, ALU.mult)\
                        .then_inc(ml_k.sem, 1)
                dve.wait_ge(*ml_k.at(l, 2))
                nc.vector.tensor_tensor_scan(g_m[0:64, :], g_lf[0:64, :], g_ig[:, :], 0.0, ALU.add, ALU.max)
                own(nc.vector.tensor_tensor_scan(g_b[:, :], resets[:, :], g_lf[0:64, :], 0.0, ALU.mult, ALU.add))
                dve.memset(MPREV[:, 0:1], 0.0)
                cp(MPREV[:, 1:NC], g_m[0:64, C - 1:T - 1:C])
                own(tt(g_ig[:, :], g_ig[:, :], g_b[:, :], ALU.subtract))
                own(tt(g_b[:, :], g_b[:, :], g_m[0:64, :], ALU.subtract))

                def chunks(ap):
                    return ap.rearrange("p (i c) -> p i c", c=C)

                tt(chunks(g_lf[0:64, :]), chunks(g_b[:, :]), MPREV[:, :].unsqueeze(2).broadcast_to([64, NC, C]), ALU.add)
                ts(g_m[0:64, :], g_m[0:64, :], -1.0, 88.0, ALU.mult, ALU.min)
                tt(chunks(g_e[:, :]), chunks(g_ig[:, :]), g_b[:, C - 1::C].unsqueeze(2).broadcast_to([64, NC, C]),
                   ALU.add).then_inc(g_rows.sem, 1)
                dve.wait_ge(*gc_mm.at(l, 1))
                cp(GC[:, :, :], PS[:, 4, 0:4 * NC].rearrange("p (q s) -> p q s", q=4)).then_inc(gc_done.sem, 1)
                dve.wait_ge(*v1_done.at(l, NC))
                dve.wait_ge(*qz_done.at(l, 4))
                for d in range(2):
                    last = dve.memset(Cst[d][:, :, 0, :], 0.0)
                own(last)
                dve.wait_ge(*gcol_done.at(l, NC))

                def decayed_keys(u):
                    s, d = u // 2, u % 2
                    ch = ORDER[d][s]
                    dve.wait_ge(*kT.at(l, u + 1))
                    if u >= 2:
                        dve.wait_ge(*kv.at(l, u - 1))
                    tt(kE[:, d, :].rearrange("p (h e) -> p h e", h=4), PS[:, 5 + d, 0:256].rearrange("p (h e) -> p h e", h=4),
                       GCOL[:, ch, 1, d, :].unsqueeze(2).broadcast_to([P, 4, HD]), ALU.mult).then_inc(kE_done.sem, 1)

                def states(u):
                    s, d = u // 2, u % 2
                    dve.wait_ge(*kv.at(l, u + 1))
                    if u >= 2:
                        dve.wait_ge(*cst_done.at(l, u - 1))
                    for t in range(2):
                        last = stt(Cst[d][:, t, s + 1, :], Cst[d][:, t, s, :], GC[:, 2 * d + t, s:s + 1],
                                   PS[:, 7 if d == 0 else 4, t * (HD + 1):(t + 1) * (HD + 1)], ALU.mult, ALU.add)
                    last.then_inc(cst_done.sem, 1)

                dve.wait_ge(*gc_done.at(l, 1))
                decayed_keys(0)
                for u in range(10):
                    if u < 9:
                        decayed_keys(u + 1)
                    states(u)
                dve.wait_ge(*o_exp.at(l, 1))
                dve.wait_ge(*cst_done.at(l, 10))

                def arguments(r):
                    i = i0 + r
                    for d in range(2):
                        dve.wait_ge(*m_a.at(l, 2 * r + d + 1))
                        if r >= 2:
                            dve.wait_ge(*m_num.at(l, 2 * (r - 1)))
                        for h in range(4):
                            last = stt(DD[r % 2][:, d, h * C:h * C + C], PS[:, 1 + d, h * C:h * C + C],
                                       GCOL[:, i, 0, d, h:h + 1], const(K_MASK + d * C, C), ALU.add, ALU.add)
                        last.then_inc(m_arg.sem, 1)

                arguments(0)
                for i in range(i0, NC):
                    r = i - i0
                    for d in range(2):
                        dve.wait_ge(*m_g.at(l, 2 * r + d + 1))
                        if r:
                            dve.wait_ge(*m_num.at(l, 2 * r))
                        tt(qG[d][:, :].rearrange("p (h c) -> p h c", h=4), qz[:, :, tok(i)],
                           PS[:, 3 + d, :].rearrange("p (h c) -> p h c", h=4), ALU.mult).then_inc(m_qg.sem, 1)
                    dve.wait_ge(*m_scores.at(l, r + 1))
                    for d in range(2):
                        dve.wait_ge(*m_dexp.at(l, 2 * r + d + 1))
                        tt(DD[r % 2][:, d, :], PS[:, 0, :], DD[r % 2][:, d, :], ALU.mult).then_inc(m_ds.sem, 1)
                    if i + 1 < NC:
                        arguments(r + 1)
                    dve.wait_ge(*m_num.at(l, 2 * r + 2))
                    num = PS[:, 3:5, 0:4 * (HD + 1)].rearrange("p d (h e) -> p d h e", h=4)
                    own(tt(DEN[:, 0, :, :], num[:, :, :, HD:HD + 1].squeeze(3), GCOL[:, i, 2, :, :], ALU.max))
                    own(stt(DEN[:, 1, :, :], num[:, :, :, HD:HD + 1].squeeze(3), -1.0, DEN[:, 0, :, :], ALU.mult, ALU.max))
                    own(nc.vector.reciprocal(DEN[:, 1, :, :], DEN[:, 1, :, :]))
                    if r:
                        dve.wait_ge(*m_turned.at(l, r))
                    for d in range(2):
                        tt(HN[:, d, :].rearrange("p (h e) -> p h e", h=4), num[:, d, :, 0:HD],
                           DEN[:, 1, d, :].unsqueeze(2).broadcast_to([P, 4, HD]), ALU.mult).then_inc(m_read.sem, 1)
                    dve.wait_ge(*m_read.at(l, 2 * r + 2))
                    tt(HN[:, 0, :], HN[:, 0, :], HN[:, 1, :], ALU.add).then_inc(m_rows.sem, 1)
                    dve.wait_ge(*m_turned.at(l, r + 1))
                    tt(PT_[:, MO:MO + 2, tok(i)], PS[:, 5, 0:256].rearrange("p (t c) -> p t c", t=2),
                       PT_[:, MO:MO + 2, tok(i)], ALU.mult).then_inc(m_out.sem, 1)
                dve.wait_ge(*m_out.at(l, NC - i0))

            def hgrn(l):
                i0 = 0 if l == 0 else 2
                f = pyramid[0]
                dve.wait_ge(*z_exp.at(l, 1))
                for q in range(4):
                    last = ts(f[:, q * T:q * T + T], f[:, q * T:q * T + T], LB1[:, l, q:q + 1], LB[:, l, q:q + 1],
                              ALU.mult, ALU.add)
                own(last)
                own(ts(Kfb[:, :, :].rearrange("p d n -> p (d n)"), f[:, :], -1.0, 1.0, ALU.mult, ALU.add))
                q2 = PT_[:, HQ:HQ + 2, :].rearrange("p t n -> p (t n)")
                for d in range(2):
                    tt(Qfb[:, d, :], q2, f[:, 2 * d * T:2 * d * T + 2 * T], ALU.mult)
                tt(Kc[:, :], Kfb[:, 0, :], Kfb[:, 1, :], ALU.add).then_inc(h_f.sem, 1)
                dve.wait_ge(*h_f.at(l, 1))

                def masked(e):
                    dve.wait_ge(*h_scores.at(l, e + 1))
                    n = NC - i0
                    dst = A[:, i0:NC, :, :].rearrange("p i h c -> p (i h) c")
                    src = PS[:, i0:NC, :].rearrange("p i (h c) -> p (i h) c", h=4)
                    nc.vector.copy_predicated(dst, M8[:, e, :].unsqueeze(1).broadcast_to([P, 4 * n, C]), src)\
                        .then_inc(h_masked.sem, 1)

                masked(0)
                for lv in range(LEVELS):
                    b = 1 << lv
                    dve.wait_ge(*h_copied.at(l, lv + 2))
                    if lv:
                        dve.wait_ge(*h_updated.at(l, lv))

                    def halves(ap, side):
                        return ap.rearrange("p (n two b) -> p n two b", two=2, b=b)[:, :, side, :]

                    nb = T // b

                    def total(d, side):
                        p_ = pyramid[lv][:, d * (2 * T >> lv):(d + 1) * (2 * T >> lv)]
                        return p_.rearrange("p (n two) -> p n two", two=2)[:, :, side:side + 1].broadcast_to([P, nb, b])

                    for arr, d, side in ((Qfb, 0, 1), (Qfb, 1, 0), (Kfb, 0, 0), (Kfb, 1, 1)):
                        tt(halves(arr[:, d, :], side), halves(arr[:, d, :], side), total(d, 1 - side), ALU.mult)
                    pair = pyramid[lv][:, :].rearrange("p (n two) -> p n two", two=2)
                    tt(pyramid[lv + 1][:, :], pair[:, :, 0], pair[:, :, 1], ALU.mult).then_inc(h_updated.sem, 1)
                    masked(lv + 1)
                dve.wait_ge(*h_updated.at(l, 7))
                dve.wait_ge(*sst_zero.at(l, 1))
                T7 = pyramid[LEVELS]
                for u in range(10):
                    s, d = u // 2, u % 2
                    dve.wait_ge(*hkv.at(l, u + 1))
                    if u >= 2:
                        dve.wait_ge(*sst_done.at(l, u - 1))
                    for t in range(2):
                        for pr in range(2):
                            rows = slice(64 * pr, 64 * pr + 64)
                            col = (2 * d + t) * NC + ORDER[d][s]
                            last = stt(Sst[rows, d, t, s + 1, 64 * pr:64 * pr + 64], Sst[rows, d, t, s, 64 * pr:64 * pr + 64],
                                       T7[rows, col:col + 1], PS[rows, 2 + d, t * P + 64 * pr:t * P + 64 * pr + 64],
                                       ALU.mult, ALU.add)
                    last.then_inc(sst_done.sem, 1)
                dve.wait_ge(*hkT.at(l, 10))
                ts(hsg[:, :, :], PT_[:, HG:HG + 2, :], -41.0, None, ALU.max).then_inc(g_clamped.sem, 1)
                dve.wait_ge(*g_silu_exp.at(l, 1))
                tt(hsg[:, :, :], hsg[:, :, :], PT_[:, HG:HG + 2, :], ALU.mult)
                t0 = i0 * C
                dve.wait_ge(*h_rs.at(l, 2))
                for t in range(2):
                    last = stt(PT_[:, HQ + t, t0:T], PT_[:, HQ + t, t0:T], par(V_HN + l), hrs[:, t, t0:T], ALU.mult,
                               ALU.mult)
                own(last)
                tt(PT_[:, HQ:HQ + 2, t0:T], PT_[:, HQ:HQ + 2, t0:T], hsg[:, :, t0:T], ALU.mult).then_inc(hg_done.sem, 1)

            def attention(l):
                for j in range(5):
                    dve.wait_ge(*a_rs.at(l, j + 1))
                    g = par((V_QN if j < 4 else V_KN) + l)
                    stt(PT_[:, AQ + j, :], PT_[:, AQ + j, :], g, ars[:, j % 2, :], ALU.mult, ALU.mult)\
                        .then_inc(a_norm.sem, 1)
                for j in range(5):
                    dve.wait_ge(*a_rot.at(l, j + 1))
                    tt(rt[:, j % 2, :], PS[:, 4 + j % 2, :], const(K_SIN, LAT), ALU.mult).then_inc(a_sin.sem, 1)
                    own(tt(PT_[:, AQ + j, CTX:T], PT_[:, AQ + j, CTX:T], const(K_COS, LAT), ALU.mult))
                    tt(PT_[:, AQ + j, CTX:T], PT_[:, AQ + j, CTX:T], rt[:, j % 2, :], ALU.add).then_inc(a_rope.sem, 1)
                units, prods = attn_units(l)

                def negmax(u):
                    h, q, nk, _ = units[u]
                    dve.wait_ge(*a_s.at(l, u + 1))
                    if u >= 2:
                        dve.wait_ge(*a_exp.at(l, u - 1))
                    a = 2 * (u % 2)
                    if nk > 4:
                        src = PS[:, a:a + 2, :].rearrange("p b n -> p (b n)")[:, 0:nk * C]
                    else:
                        src = PS[:, a, 0:nk * C]
                    nc.vector.tensor_reduce(NEGM[:, u % 2:u % 2 + 1], src, AX.X, ALU.max, negate=True)\
                        .then_inc(a_max.sem, 1)

                def scaled(u):
                    h, q, nk, pr = units[u]
                    dve.wait_ge(*a_exp.at(l, u + 1))
                    own(nc.vector.reciprocal(PSUMS[:, 2 + u % 2:3 + u % 2], PSUMS[:, u % 2:u % 2 + 1]))
                    ts(Pb[:, u % 2, 0:nk * C], Pb[:, u % 2, 0:nk * C], PSUMS[:, 2 + u % 2:3 + u % 2], None, ALU.mult)\
                        .then_inc(a_scaled.sem, 1)

                def turned(u):
                    h, q, nk, pr = units[u]
                    q0 = prods[pr][1]
                    if u % 2 == 0:
                        return
                    dve.wait_ge(*a_T.at(l, u + 1))
                    if pr >= 2:
                        dve.wait_ge(*a_pv.at(l, pr - 1))
                    src = PS[:, 4:6, :].rearrange("p b n -> p (b n)")[:, 0:nk * C]
                    cp(PTr[:, pr % 2, 0:nk, (q - q0) * C:(q - q0) * C + C],
                       src.rearrange("p (k c) -> p k c", k=nk)).then_inc(a_Tdve.sem, 1)

                negmax(0)
                for u in range(len(units)):
                    scaled(u)
                    if u + 1 < len(units):
                        negmax(u + 1)
                    turned(u)

            for l in range(DEPTH):
                n_in, n_out, n_ff = slots(l)
                if l == 0:
                    low(0, 0)
                    dve.wait_ge(*wg_high.at(l, 1))
                    tt(wg_lo[:, :, :], wg_raw[:, :, :], wg_hi[:, :, :].bitcast(F32), ALU.subtract).then_inc(wg_low.sem, 1)
                u_parts(l, 0, SEGS)
                if l:
                    dve.wait_ge(*wg_high.at(l, 1))
                    tt(wg_lo[:, :, :], wg_raw[:, :, :], wg_hi[:, :, :].bitcast(F32), ALU.subtract).then_inc(wg_low.sem, 1)
                with dve.Fori(0, 6) as i:
                    for j in range(4):
                        low(n_in + i * 4 + j + 1, j + 1)
                mlstm(l)
                hgrn(l)
                attention(l)
                s0 = segs(l)[0][0]
                dve.wait_ge(*a_out.at(l, len(attn_units(l)[1])))
                for k in range(DK):
                    src = AO[:, k, s0:T] if k < 4 else PT_[:, (HQ if k < 6 else MO) + k % 2, s0:T]
                    dve.wait_ge(*u_high.at(l, 9 + k))
                    tt(Ul[:, k, s0:T], src, Uh[:, k, s0:T].bitcast(F32), ALU.subtract).then_inc(u_ready.sem, 1)

                def add_to_residual(j, gate_row, g=None):
                    for bank, (t0, tn) in enumerate(SEGS):
                        if (t0, tn) in segs(l):
                            who = 1 if t0 == 0 else 0
                            last = stt(H[:, j, t0:t0 + tn], PS[:, 2 * (j % 2) + bank, 0:tn],
                                       MOD[:, l, gate_row + j, who:who + 1], H[:, j, t0:t0 + tn], ALU.mult, ALU.add)
                    last.then_inc(evac_dve.sem, 1)

                for j in range(8):
                    low(n_out + j + 1, j + 1)
                    dve.wait_ge(gemm.sem, n_out + j + 1)
                    add_to_residual(j, 16)
                dve.wait_ge(*evac_dve.at(l, 8))
                u_parts(l, 1, segs(l))

                def mlp(g, last_group=False):
                    for j in range(8):
                        low(n_ff + g * 16 + j + 1, j + 1)
                        t0 = segs(l)[0][0]
                        f = 32 * l + g * 8 + j
                        dve.wait_ge(evac_act.sem, 56 * l + 24 + g * 8 + j + 1)
                        if not isinstance(f, int) or f >= 2:
                            dve.wait_ge(hid_ready.sem, f - 1)
                        tt(hsq[:, j % 2, t0:T], relu[:, j % 2, t0:T], relu[:, j % 2, t0:T], ALU.mult)\
                            .then_inc(hid_square.sem, 1)
                        dve.wait_ge(hid_square.sem, f + 1)
                        dve.wait_ge(hid_high.sem, f + 1)
                        tt(hidl[:, j, t0:T], hsq[:, j % 2, t0:T], hidh[:, j, t0:T].bitcast(F32), ALU.subtract)\
                            .then_inc(hid_ready.sem, 1)
                    for j in range(8):
                        if not (last_group and j == 7):
                            low(n_ff + g * 16 + 8 + j + 1, j + 1)
                        dve.wait_ge(gemm.sem, n_ff + g * 16 + 8 + j + 1)
                        if j == 0:
                            dve.wait_ge(evac_dve.sem, 40 * l + 8 + g * 8)
                        add_to_residual(j, 40)

                if l == 0:
                    mlp(0)
                    with dve.Fori(1, FG) as g:
                        mlp(g)
                else:
                    with dve.Fori(0, FG - 1) as g:
                        mlp(g)
                    mlp(FG - 1, True)
            for i in range(4):
                dve.wait_ge(out_T.sem, 2 * i + 2)
                cp(onat[:, i, 512:1024], PS[:, 5 + 2 * (i % 2), :]).then_inc(out_dve.sem, 1)


_INS = ['x', 'c', 'ctx', 'c_ctx', 'w_mod', 'b_mod', 'norm_mix', 'norm_ffn', 'w_in', 'b_in', 'q_norm', 'k_norm',
        'hg_lb', 'hg_norm', 'ml_conv', 'w_out', 'w_ff1', 'w_ff2']


def kernel(**inputs):
    import numpy as _np
    import concourse.bacc as _bacc
    from concourse import mybir as _mybir
    from concourse.bass_utils import run_bass_kernel_spmd as _run

    nc = _bacc.Bacc("TRN2", target_bir_lowering=False, num_devices=1)
    arrays, args = {}, []
    k, m = tables()
    for name, a in [(n, inputs[n]) for n in _INS] + [("constants", k), ("level_masks", m)]:
        a = _np.ascontiguousarray(a)
        arrays[f"in_{name}_dram"] = a
        args.append(nc.dram_tensor(f"in_{name}_dram", a.shape, _mybir.dt.from_np(a.dtype), kind="ExternalInput").ap())
    args.append(nc.dram_tensor("out_0_dram", (1, LAT, D), F32, kind="ExternalOutput").ap())
    hybrid_dit_block(nc, *args)
    r = _run(nc, [arrays], core_ids=[0])
    return r.results[0]["out_0_dram"]
```

```python
from contextlib import ExitStack

import numpy as np

import concourse.bass as bass
from concourse import mybir

F32 = mybir.dt.float32
F32R = mybir.dt.float32r
U8 = mybir.dt.uint8
ALU = mybir.AluOpType
ACT = mybir.ActivationFunctionType
AX = mybir.AxisListType

P = 128
D = 1024
DK = D // P
CTX = 256
LAT = 512
T = CTX + LAT
DEPTH = 2
HD = 64
C = 128
NC = T // C
EPS = 1e-6
N_IN = 3088
IN_TILES = 24
FF = 4096
FG = 4
SEGS = ((0, CTX), (CTX, LAT))
AQ, AK, AV, HQ, HV, HZ, HG, MQ, MK, MV, MO, GT = 0, 4, 5, 6, 8, 10, 14, 16, 18, 20, 22, 24
MOD_GROUPS = 24
EARLY = 4
LATE_FIRST = (3, 2)
LATE_AFTER = (12, 20)
LEVELS = 7
ORDER = (tuple(range(NC)), (1, 0, 5, 4, 3, 2))
STEP = tuple(tuple(o.index(c) for c in range(NC)) for o in ORDER)

IN_ORDER = (18, 19, 20, 21, 16, 17, 22, 23, 8, 9, 10, 11, 12, 13, 4, 5, 6, 7, 14, 15, 0, 1, 2, 3)
LAT_GROUPS = (1, 4, 5)
K_ID, K_ROT, K_COS, K_SIN, K_KZ, K_BLK, K_ONE, K_HM, K_MASK, K_SEL, K_PAIR = (
    0, 128, 256, 768, 1280, 1792, 1920, 2048, 2050, 2306, 3330)
K_N = 3842
V_BMOD, V_NMIX, V_NFFN, V_BIN, V_LB, V_CONV, V_QN, V_KN, V_HN, V_C = 0, 96, 112, 128, 176, 184, 208, 210, 212, 214
V_N = 230


def tables():
    k = np.zeros((P, K_N), np.float32)
    k[:, K_ID:K_ID + P] = np.eye(P)
    for base in range(0, P, 32):
        for i in range(16):
            k[base + 16 + i, K_ROT + base + i] = -1.0
            k[base + i, K_ROT + base + 16 + i] = 1.0
    half = HD // 2
    inv = (np.float32(10000.0) ** (-np.arange(0, half, 2, dtype=np.float32) / np.float32(half))).astype(np.float32)
    tok = np.arange(LAT)
    row = (tok // 64).astype(np.float32)[None, :] * inv[:, None]
    col = (tok % 64).astype(np.float32)[None, :] * inv[:, None]
    ang = np.concatenate([row, row, col, col] * 2, axis=0)
    k[:, K_COS:K_COS + LAT] = np.cos(ang)
    k[:, K_SIN:K_SIN + LAT] = np.sin(ang)
    for g in range(2):
        for par in range(2):
            for d in range(HD):
                k[64 * g + d, K_KZ + (2 * g + par) * P + 64 * par + d] = 1.0
    for b in range(2):
        k[64 * b:64 * b + 64, K_BLK + 64 * b:K_BLK + 64 * b + 64] = 1.0 / HD
        k[64 * b:64 * b + 64, K_HM + b] = 1.0
    k[:, K_ONE:K_ONE + P] = 1.0 / D
    s, t = np.arange(C)[:, None], np.arange(C)[None, :]
    k[:, K_MASK:K_MASK + C] = np.where(s <= t, 0.0, -1e30)
    k[:, K_MASK + C:K_MASK + 2 * C] = np.where(s >= t, 0.0, -1e30)
    for d in range(2):
        for h in range(4):
            k[32 * d + h, K_SEL + (4 * d + h) * P:K_SEL + (4 * d + h + 1) * P] = 1.0
        for tt in range(2):
            for par in range(2):
                at = K_PAIR + (2 * d + tt) * P + 64 * par
                k[32 * d + 2 * tt + par, at:at + 64] = 1.0
    m = np.zeros((P, LEVELS + 1, C), np.float32)
    m[:, 0] = s == t
    for lv in range(LEVELS):
        b = 2 << lv
        m[:, lv + 1] = (s // b == t // b) & (s // (b // 2) != t // (b // 2))
    return k, m



class Signal:

    def __init__(self, sem, per_layer=0):
        self.sem, self.per_layer = sem, per_layer

    def at(self, layer, n):
        return self.sem, layer * self.per_layer + n


def hybrid_dit_block(nc: bass.Bass, x, c, ctx_in, c_ctx, w_mod, b_mod, norm_mix, norm_ffn, w_in, b_in, q_norm, k_norm,
                     hg_lb, hg_norm, ml_conv, w_out, w_ff1, w_ff2, consts, level_masks, out):
    with ExitStack() as es:
        base = 16512
        slot = T
        W_H, W_U, W_P = 0, 8 * slot, 24 * slot
        W_RAW = 49 * slot
        W_HI, W_LO = W_RAW + 4096, W_RAW + 4096 + 2048
        W_K = W_LO + 2048
        W_M8 = W_K + K_N + 6
        W_X = W_M8 + 256

        def at(name, shape, word, dt=F32):
            return nc.alloc_sbuf_tensor_at(name, shape, dt, offset=base + 4 * word)

        def u_at(n):
            return W_U + n * slot

        def p_at(n):
            return W_P + n * slot

        H = at("residual", [P, DK, T], W_H)
        Uh = at("u_high", [P, DK, T], u_at(0), F32R)
        Ul = at("u_low", [P, DK, T], u_at(8), F32R)
        PT_ = at("projections", [P, 25, T], p_at(0))
        raw = at("weights_raw", [P, 4, DK, P], W_RAW)
        whi = at("weights_high", [P, 2, DK, P], W_HI, F32R)
        wlo = at("weights_low", [P, 2, DK, P], W_LO, F32R)
        K = at("constants", [P, K_N], W_K)
        M8 = at("level_masks", [P, LEVELS + 1, C], W_M8, U8)
        V = at("parameters", [P, V_N], W_X + 0)
        MOD = at("modulation", [P, DEPTH, 48, 2], W_X + 232)
        GAIN = at("norm_gains", [P, DEPTH, 2, DK, 2], W_X + 424)
        GB = at("gate_bias", [P, DEPTH], W_X + 488)
        LBT = at("lb_work", [P, 5, 4], W_X + 496)
        LB = at("lower_bounds", [P, DEPTH, 4], W_X + 520)
        LB1 = at("one_minus_lower_bounds", [P, DEPTH, 4], W_X + 528)
        EPST = at("epsilon", [P, 2], W_X + 536)
        GCOL = at("gate_columns", [P, NC, 3, 2, 4], W_X + 544)
        GC = at("chunk_decays", [P, 4, NC], W_X + 688)
        MPREV = at("max_before_chunk", [64, NC], W_X + 712)
        CS = at("silu_c", [P, DK, 2], W_X + 720)
        NEGM = at("minus_row_max", [P, 8], W_X + 736)
        DEN = at("denominators", [P, 2, 2, 4], W_X + 744)
        HN = at("mlstm_rows", [P, 2, 4 * HD], W_X + 760)
        PSUMS = at("prob_sums", [P, 4], W_X + 1272)
        late_row_buf = at("late_modulation_rows", [2, 512], W_X + 1280)
        assert base + 4 * (W_X + 1792) <= nc.sbuf_usable_end

        modrow = at("modulation_rows", [2, EARLY * 512], p_at(0))
        xnat = at("tokens_natural", [P, NC, D], p_at(16))
        vrow = at("parameter_rows", [P, 2, P], p_at(24))
        wm = at("w_mod_ring", [P, 3, DK, 512], u_at(0))
        mask_in = at("level_masks_in", [P, LEVELS + 1, C], W_LO)
        wml = at("w_mod_late_ring", [P, 3, 2, 512], W_RAW + 1024)
        sqb = at("squares", [P, 2, T], p_at(20))
        rsb = at("inverse_rms", [P, T], p_at(22))
        tb = at("scaled", [P, 2, T], p_at(23))
        wg_raw = at("gate_weights", [P, DK, P], p_at(12))
        wg_hi = at("gate_weights_high", [P, DK, P], p_at(12) + 1024, F32R)
        wg_lo = at("gate_weights_low", [P, DK, P], p_at(12) + 2048, F32R)
        hidh = at("hidden_high", [P, DK, T], p_at(0), F32R)
        hidl = at("hidden_low", [P, DK, T], p_at(8), F32R)
        relu = at("hidden_relu", [P, 2, T], p_at(16))
        hsq = at("hidden_square", [P, 2, T], p_at(18))
        Y = at("conv", [P, 4, T], p_at(0))
        DD = [at("decay_scores_0", [P, 2, 4 * C], u_at(0)), at("decay_scores_1", [P, 2, 4 * C], u_at(8) + 1568)]
        qG0 = at("q_decayed_fwd", [P, 4 * C], u_at(0) + 1024)
        g_b = at("gate_cumsum", [64, T], u_at(2))
        g_e = at("gate_key_decay", [64, T], u_at(3))
        qz = at("q_one_head", [P, 4, T], u_at(4))
        V1 = at("v_and_ones", [P, NC, 4, HD + 1], u_at(8))
        g_lf = at("gate_forget", [P, T], u_at(12))
        g_ig = at("gate_input", [64, T], u_at(13))
        g_m = at("gate_max", [P, T], u_at(14))
        resets = at("chunk_resets", [64, T], u_at(15))
        qG1 = at("q_decayed_bwd", [P, 4 * C], u_at(15))
        kE = at("k_decayed", [P, 2, 4 * HD], u_at(0))
        Cst = [at(f"mlstm_states_{d}", [P, 2, NC, HD + 1], p_at(16 + 4 * d)) for d in range(2)]
        qG = [qG0, qG1]
        Qfb = at("q_decayed", [P, 2, 2 * T], u_at(0))
        Kfb = at("k_decayed_hg", [P, 2, 2 * T], u_at(4))
        Qc = [at(f"q_level_{r}", [P, 2 * T], u_at(8 + 2 * r)) for r in range(2)]
        Kc = [at("k_level_0", [P, 2 * T], u_at(12)), at("k_level_1", [P, 2 * T], p_at(HQ))]
        A = at("scores", [P, 2, NC, 2, C], p_at(16))
        pyramid = [PT_[:, HZ:HZ + 4, :].rearrange("p t n -> p (t n)"), at("forget_2", [P, 2 * T], u_at(14))]
        word = p_at(20)
        for lv in range(2, LEVELS + 1):
            pyramid.append(at(f"forget_{1 << lv}", [P, 4 * T >> lv], word))
            word += 4 * T >> lv
        Vz = at("v_one_head", [P, NC, 4, P], p_at(HZ))
        Sst = at("hg_states", [P, 2, 2, NC, P], u_at(8))
        kn = at("k_natural", [P, 2, 2, P], u_at(12))
        hsqr = at("hg_squares", [P, 2, T], u_at(0))
        hrs = at("hg_inverse_rms", [P, 2, T], u_at(2))
        hsg = at("hg_silu_gate", [P, 2, T], u_at(4))
        kz = at("k_one_half", [P, 4, T], u_at(0))
        Va = at("attn_v", [P, NC, P], u_at(4))
        PTr = at("probs_transposed", [P, 2, NC, LAT], u_at(6))
        Pb = at("probs", [P, 2, T], u_at(14))
        AO = at("attn_out", [P, 4, T], p_at(8))
        asq = at("attn_squares", [P, 2, T], p_at(12))
        ars = at("attn_inverse_rms", [P, 2, T], p_at(14))
        rt = at("rope_sin_part", [P, 2, LAT], p_at(18))
        onat = at("out_rows", [P, 4, D], p_at(0))

        PS = es.enter_context(nc.psum_tensor("psum", [P, 8, 512], F32))

        sems = {}

        def signal(name, per_layer=0):
            s = Signal(es.enter_context(nc.semaphore(name)), per_layer)
            sems[name] = s
            return s

        const_loaded = signal("const_loaded")
        x_loaded = signal("x_loaded")
        gate_bias_zero = signal("gate_bias_zero")
        wm_loaded = [signal(f"wm_loaded_{r}") for r in range(3)]
        par_T = signal("par_T")
        par_ready = signal("par_ready")
        c_exp = signal("c_exp")
        c_silu = signal("c_silu")
        x_T = signal("x_T")
        x_act = signal("x_act")
        x_dve = signal("x_dve")
        mod_mm = signal("mod_mm")
        mod_row = signal("mod_row")
        mod_T = signal("mod_T")
        mod_ready = signal("mod_ready")
        wml_loaded = [signal(f"wml_loaded_{r}") for r in range(3)]
        late_part = signal("late_part")
        late_row = signal("late_row")
        late_turned = signal("late_turned")
        late_taken = signal("late_taken")
        late_ready = signal("late_ready")
        lb_exp = signal("lb_exp")
        lb_max = signal("lb_max")
        dve_step = signal("dve_step")
        act_step = signal("act_step")
        pool_step = signal("pool_step")

        w_loaded = [signal(f"w_loaded_{r}") for r in range(4)]
        w_high = signal("w_high", 96)
        w_low = signal("w_low", 96)
        gemm = signal("gemm", 96)
        evac_act = signal("evac_act", 56)
        evac_dve = signal("evac_dve", 40)
        u_high = signal("u_high_ready", 24)
        u_ready = signal("u_ready", 24)
        n_square = signal("n_square", 16)
        n_sum = signal("n_sum", 16)
        n_stat = signal("n_stat", 2)
        n_rs = signal("n_rs", 2)
        n_scaled = signal("n_scaled", 16)
        hid_high = signal("hid_high", 32)
        hid_square = signal("hid_square", 32)
        hid_ready = signal("hid_ready", 32)

        wg_loaded = signal("wg_loaded", 64)
        wg_high = signal("wg_high_ready", 1)
        wg_low = signal("wg_low_ready", 1)
        gate_mm = signal("gate_mm", 1)
        gate_tok = signal("gate_tok", 1)

        conv_done = signal("conv_done", 4)
        ml_exp = signal("ml_exp", 4)
        ml_q = signal("ml_q", 2)
        ml_k = signal("ml_k", 2)
        qz_done = signal("qz_done", 4)
        g_softplus = signal("g_softplus", 1)
        g_rows = signal("g_rows", 1)
        g_exp = signal("g_exp", 1)
        v1_ones = signal("v1_ones", 1)
        vT = signal("vT", NC)
        v1_done = signal("v1_done", NC)
        gT = signal("gT", NC)
        gcol_done = signal("gcol_done", NC)
        gc_mm = signal("gc_mm", 1)
        gc_done = signal("gc_done", 1)
        kT = signal("kT", 10)
        kE_done = signal("kE_done", 10)
        kv = signal("kv", 10)
        cst_done = signal("cst_done", 10)
        o_exp = signal("o_exp", 2)
        ctx_zero = signal("ctx_zero", 0)
        m_scores = signal("m_scores", 6)
        m_a = signal("m_a", 12)
        m_g = signal("m_g", 12)
        m_arg = signal("m_arg", 12)
        m_qg = signal("m_qg", 12)
        m_dexp = signal("m_dexp", 12)
        m_rows = signal("m_rows", 6)
        m_turned = signal("m_turned", 6)
        m_read = signal("m_read", 12)
        o_clamped = signal("o_clamped", 1)
        z_clamped = signal("z_clamped", 1)
        g_clamped = signal("g_clamped", 1)
        m_ds = signal("m_ds", 12)
        m_num = signal("m_num", 12)
        m_out = signal("m_out", 6)

        z_exp = signal("z_exp", 4)
        forget = signal("forget", 4)
        h_f = signal("h_f", 1)
        h_copied = signal("h_copied", 8)
        h_scores = signal("h_scores", 16)
        h_masked = signal("h_masked", 16)
        h_updated = signal("h_updated", 7)
        vz_zero = signal("vz_zero", 1)
        sst_zero = signal("sst_zero", 1)
        hvT = signal("hvT", NC)
        vz_done = signal("vz_done", NC)
        hkT = signal("hkT", 10)
        kn_done = signal("kn_done", 10)
        hkv = signal("hkv", 10)
        sst_done = signal("sst_done", 10)
        h_o = signal("h_o", 6)
        h_oe = signal("h_oe", 6)
        h_sq = signal("h_sq", 2)
        h_ms = signal("h_ms", 2)
        h_rs = signal("h_rs", 2)
        g_silu_exp = signal("g_silu_exp", 1)
        hg_done = signal("hg_done", 1)

        a_sq = signal("a_sq", 5)
        a_ms = signal("a_ms", 5)
        a_rs = signal("a_rs", 5)
        a_norm = signal("a_norm", 5)
        a_rot = signal("a_rot", 5)
        a_sin = signal("a_sin", 5)
        a_rope = signal("a_rope", 5)
        kz_mm = signal("kz_mm", 4)
        kz_done = signal("kz_done", 4)
        avT = signal("avT", NC)
        va_done = signal("va_done", NC)
        NU0 = 8 * 6
        a_s = signal("a_s", NU0)
        a_max = signal("a_max", NU0)
        a_exp = signal("a_exp", NU0)
        a_T = signal("a_T", NU0)
        a_Tact = signal("a_Tact", NU0 // 2)
        a_Tdve = signal("a_Tdve", NU0 // 2)
        a_pv = signal("a_pv", 16)
        a_scaled = signal("a_scaled", NU0)
        a_out = signal("a_out", 16)
        out_T = signal("out_T")
        out_act = signal("out_act")
        out_dve = signal("out_dve")
        stored = signal("stored")

        def const(col, n, rows=P):
            return K[0:rows, col:col + n]

        def tok(i):
            return slice(i * C, (i + 1) * C)

        ident = const(K_ID, P)

        def par(col, n=1):
            return V[:, col:col + n]

        def slots(l):
            return 96 * l, 96 * l + 24, 96 * l + 32

        def segs(l):
            return SEGS if l == 0 else SEGS[1:]

        def attn_units(l):
            units, prods = [], []
            for h in range(8):
                if l == 0:
                    units += [(h, q, 2, len(prods)) for q in range(2)]
                    prods.append((h, 0, 2, 2))
                units += [(h, 2 + q, NC, len(prods)) for q in range(4)]
                prods.append((h, 2, 4, NC))
            return units, prods

        def turned_at(l, u):
            return (a_Tdve if u % 2 else a_Tact).at(l, u // 2 + 1)

        block = es.enter_context(nc.Block())

        @block.sync
        def _(sp):
            def load(n, j, src):
                if not isinstance(n, int) or n >= 4:
                    sp.wait_ge(w_high.sem, n - 3)
                    sp.wait_ge(w_low.sem, n - 3)
                sp.dma_start(raw[:, j % 4, :, :], src).then_inc(w_loaded[j % 4].sem, 16)

            sp.dma_start(K[:, :], consts).then_inc(const_loaded.sem, 16)
            sp.dma_start(mask_in[:, :, :], level_masks).then_inc(const_loaded.sem, 16)
            sp.dma_start(vrow[0:96, 0, :], b_mod.rearrange("l (r c) -> (l r) c", c=P)).then_inc(const_loaded.sem, 16)
            sp.dma_start(vrow[96:112, 0, :], norm_mix.rearrange("l (r c) -> (l r) c", c=P)).then_inc(const_loaded.sem, 16)
            sp.dma_start(vrow[112:128, 0, :], norm_ffn.rearrange("l (r c) -> (l r) c", c=P)).then_inc(const_loaded.sem, 16)
            for l in range(DEPTH):
                sp.dma_start(vrow[24 * l:24 * l + 24, 1, :],
                             b_in[l, 0:3072].rearrange("(r c) -> r c", c=P)).then_inc(const_loaded.sem, 16)
            sp.dma_start(vrow[48:56, 1, :], hg_lb.rearrange("l d (t c) -> (l d t) c", c=P)).then_inc(const_loaded.sem, 16)
            sp.dma_start(vrow[56:80, 1, :], ml_conv.rearrange("l j (t c) -> (l j t) c", c=P)).then_inc(const_loaded.sem, 16)
            for row, g in ((80, q_norm), (82, k_norm), (84, hg_norm)):
                for half in range(2):
                    sp.dma_start(vrow[row:row + 2, 1, 64 * half:64 * half + 64], g).then_inc(const_loaded.sem, 16)
            sp.dma_start(vrow[86:94, 1, :], c.rearrange("a (r c) -> (a r) c", c=P)).then_inc(const_loaded.sem, 16)
            sp.dma_start(vrow[94:102, 1, :], c_ctx.rearrange("(r c) -> r c", c=P)).then_inc(const_loaded.sem, 16)
            sp.dma_start(xnat[:, 0:2, :], ctx_in.rearrange("a (i p) d -> p (a i) d", p=P)).then_inc(x_loaded.sem, 16)
            sp.dma_start(xnat[:, 2:6, :], x.rearrange("a (i p) d -> p (a i) d", p=P)).then_inc(x_loaded.sem, 16)
            for s in range(EARLY):
                if s >= 3:
                    sp.wait_ge(mod_mm.sem, s - 2)
                sp.dma_start(wm[:, s % 3, :, :],
                             w_mod[0, :, 512 * s:512 * s + 512].rearrange("(k p) m -> p k m", p=P)).then_inc(wm_loaded[s % 3].sem, 16)

            def late_loads(l):
                wmq = w_mod.rearrange("l (q k p) (g m) -> l g q p k m", q=4, p=P, m=512)

                def part(layer, g, q, p, r):
                    if not isinstance(p, int) or p >= 3:
                        sp.wait_ge(late_part.sem, p - 2)
                    sp.dma_start(wml[:, r % 3, :, :], wmq[layer, g, q]).then_inc(wml_loaded[r % 3].sem, 16)

                sp.wait_ge(*w_high.at(l, 24))
                sp.wait_ge(*w_low.at(l, 24))
                if l == 0:
                    for r in range(12):
                        part(0, EARLY + r // 4, r % 4, r, r)
                    with sp.Fori(1, 2) as i:
                        for r in range(12):
                            part(0, i * 3 + (EARLY + r // 4), r % 4, i * 12 + r, r)
                    for r in range(24, 32):
                        part(0, EARLY + r // 4, r % 4, r, r)
                    for r in range(32, 48):
                        part(1, r // 4 - 8, r % 4, r, r)
                else:
                    with sp.Fori(0, 2) as i:
                        for r in range(12):
                            part(1, i * 3 + (4 + r // 4), r % 4, i * 12 + (48 + r), r)
                    for r in range(24, 32):
                        part(1, 4 + r // 4, r % 4, 48 + r, r)
                sp.wait_ge(late_part.sem, 4 * LATE_AFTER[l])

            for l in range(DEPTH):
                n_in, n_out, n_ff = slots(l)
                win = w_in[l, :, 0:3072].rearrange("(k p) (j m) -> j p k m", p=P, m=P)
                for j in range(IN_TILES):
                    load(n_in + j, j, win[IN_ORDER[j]])
                wout = w_out[l].rearrange("(k p) (j m) -> j p k m", p=P, m=P)
                load(n_out, 0, wout[0])
                late_loads(l)
                for j in range(1, 8):
                    load(n_out + j, j, wout[j])
                w1 = w_ff1[l].rearrange("(k p) (j m) -> j p k m", p=P, m=P)
                w2 = w_ff2[l].rearrange("(g k p) (j m) -> g j p k m", p=P, k=DK, m=P)
                with sp.Fori(0, FG) as g:
                    for j in range(8):
                        load(n_ff + g * 16 + j, j, w1[g * 8 + j])
                    for j in range(8):
                        load(n_ff + g * 16 + 8 + j, j, w2[g, j])
            for i in range(4):
                sp.wait_ge(out_act.sem, i + 1)
                sp.wait_ge(out_dve.sem, i + 1)
                sp.dma_start(out[0, C * i:C * i + C, :], onat[:, i, :]).then_inc(stored.sem, 16)
            sp.wait_ge(stored.sem, 64)

        @block.gpsimd
        def _(pool):
            steps = [0]

            def own(ins):
                steps[0] += 1
                ins.then_inc(pool_step.sem, 1)
                pool.wait_ge(pool_step.sem, steps[0])

            own(pool.memset(GB[:, :], 0.0))
            for l in range(DEPTH):
                for q in range(4):
                    pool.dma_start(GB[32 * q:32 * q + 4, l:l + 1],
                                   b_in[l, 3072 + 4 * q:3076 + 4 * q].rearrange("(a b) -> a b", b=1))\
                        .then_inc(gate_bias_zero.sem, 16)
            pool.wait_ge(mod_ready.sem, 1)
            for l in range(DEPTH):
                if l:
                    pool.wait_ge(*gemm.at(l, 0))
                    pool.wait_ge(*u_ready.at(l, 1))
                own(pool.memset(wg_raw[:, :, :], 0.0))
                for q in range(4):
                    pool.dma_start(wg_raw[:, :, 32 * q:32 * q + 4],
                                   w_in[l, :, 3072 + 4 * q:3076 + 4 * q].rearrange("(k p) m -> p k m", p=P))\
                        .then_inc(wg_loaded.sem, 16)
                if l:
                    pool.wait_ge(*u_ready.at(l, 8))
                    pool.wait_ge(*gate_mm.at(l, 1))
                    for tile in (HQ, HG, MQ, MO):
                        pool.memset(PT_[:, tile:tile + 2, 0:CTX], 0.0).then_inc(ctx_zero.sem, 1)
                    pool.wait_ge(ctx_zero.sem, 4)
                for clamped, tile, n, slots_done in ((o_clamped, MO, 2, 8), (z_clamped, HZ, 4, 14)):
                    pool.wait_ge(*evac_act.at(l, slots_done))
                    pool.tensor_scalar(PT_[:, tile:tile + n, :], PT_[:, tile:tile + n, :], -41.0, 0.0, ALU.max, ALU.add)\
                        .then_inc(clamped.sem, 1)
                if l:
                    pool.wait_ge(*ml_q.at(l, 2))
                    pool.wait_ge(*ml_k.at(l, 2))
                    pool.memset(PT_[:, AQ:AQ + 4, 0:CTX], 0.0).then_inc(ctx_zero.sem, 1)
                pool.wait_ge(*gemm.at(l, 24))
                pool.memset(V1[:, :, :, HD:HD + 1], 1.0).then_inc(v1_ones.sem, 1)
                pool.wait_ge(*h_updated.at(l, 1))
                pool.memset(Vz[:, :, :, :], 0.0).then_inc(vz_zero.sem, 1)
                pool.wait_ge(*h_scores.at(l, 16))
                pool.memset(Sst[:, :, :, :, :], 0.0).then_inc(sst_zero.sem, 1)

        @block.tensor
        def _(pe):
            mm = nc.tensor.matmul
            tr = nc.tensor.transpose

            def gemm_slot(l, n, j, rhs_hi, rhs_lo, free, ss, ready=None):
                pe.wait_ge(w_low.sem, n + 1)
                if free is not None:
                    pe.wait_ge(*free)
                for k in range(DK):
                    if ready is not None:
                        pe.wait_ge(*ready(k))
                    for bank, (t0, tn) in enumerate(SEGS):
                        if (t0, tn) not in ss:
                            continue
                        o = PS[:, 2 * (j % 2) + bank, 0:tn]
                        a, b = whi[:, j % 2, k, :], wlo[:, j % 2, k, :]
                        h, lo = rhs_hi[:, k, t0:t0 + tn], rhs_lo[:, k, t0:t0 + tn]
                        mm(o, b, h, start=(k == 0), stop=False)
                        mm(o, a, lo, start=False, stop=False)
                        last = mm(o, a, h, start=False, stop=(k == DK - 1))
                last.then_inc(gemm.sem, 1)

            def stats(l, w, ss):
                pe.wait_ge(*n_sum.at(l, 8 * w + 8))
                for bank, (t0, tn) in enumerate(SEGS):
                    if (t0, tn) in ss:
                        last = mm(PS[:, 4 + bank, 0:tn], const(K_ONE, P), rsb[:, t0:t0 + tn], start=True, stop=True)
                last.then_inc(n_stat.sem, 1)

            pe.wait_ge(const_loaded.sem, 17 * 16)
            tr(PS[:, 0, 0:P], vrow[:, 0, :], ident)
            tr(PS[:, 0, P:P + 102], vrow[0:102, 1, :], ident[0:102, 0:102]).then_inc(par_T.sem, 1)
            pe.wait_ge(x_loaded.sem, 32)
            for n in range(12):
                i, half = n // 2, n % 2
                if n >= 4:
                    pe.wait_ge((x_act if n % 2 == 0 else x_dve).sem, (n - 4) // 2 + 1)
                for q in range(4):
                    k = 4 * half + q
                    last = tr(PS[:, 2 + n % 4, q * P:q * P + P], xnat[:, i, k * P:k * P + P], ident)
                last.then_inc(x_T.sem, 1)
            pe.wait_ge(c_silu.sem, 1)
            for s in range(EARLY):
                pe.wait_ge(wm_loaded[s % 3].sem, 16 * (s // 3 + 1))
                if s >= 2:
                    pe.wait_ge(mod_row.sem, s - 1)
                for k in range(DK):
                    last = mm(PS[0:2, 6 + s % 2, :], CS[:, k, :], wm[:, s % 3, k, :], start=(k == 0), stop=(k == DK - 1))
                last.then_inc(mod_mm.sem, 1)
            pe.wait_ge(mod_row.sem, EARLY)
            for m in range(4 * EARLY):
                last = mm(PS[:, 1, 2 * m:2 * m + 2], modrow[0:2, m * P:m * P + P], ident[0:2, 0:2], start=True, stop=True)
            last.then_inc(mod_T.sem, 1)

            issued = [0, 0]

            def late_turn(g):
                pe.wait_ge(late_row.sem, g + 1)
                if g:
                    pe.wait_ge(late_taken.sem, g)
                for m in range(4):
                    last = mm(PS[:, 7, 2 * m:2 * m + 2], late_row_buf[0:2, m * P:m * P + P], ident[0:2, 0:2],
                              start=True, stop=True)
                last.then_inc(late_turned.sem, 1)
                issued[1] = g + 1

            def late_parts(n):
                for p in range(issued[0], issued[0] + n):
                    g, q = divmod(p, 4)
                    if q == 0 and issued[1] < g:
                        late_turn(g - 1)
                    pe.wait_ge(wml_loaded[p % 3].sem, 16 * (p // 3 + 1))
                    for k in range(2):
                        last = mm(PS[0:2, 6, :], CS[:, 2 * q + k, :], wml[:, p % 3, k, :], start=(q == 0 and k == 0),
                                  stop=(q == 3 and k == 1))
                    last.then_inc(late_part.sem, 1)
                    issued[0] = p + 1

            def late_finish():
                late_turn(issued[0] // 4 - 1)
                pe.wait_ge(late_taken.sem, issued[1])

            def mlstm(l):
                i0 = 0 if l == 0 else 2
                for i in range(NC):
                    if i >= 2:
                        pe.wait_ge(*v1_done.at(l, i - 1))
                    if i == 0:
                        pe.wait_ge(*evac_act.at(l, 24))
                    tr(PS[:, i % 2, 0:P], PT_[:, MV, tok(i)], ident)
                    tr(PS[:, i % 2, P:2 * P], PT_[:, MV + 1, tok(i)], ident).then_inc(vT.sem, 1)
                late_parts(4 * LATE_FIRST[l])
                late_finish()
                pe.wait_ge(*g_exp.at(l, 1))
                for i in range(NC):
                    if i >= 2:
                        pe.wait_ge(*gcol_done.at(l, i - 1))
                    tr(PS[:, 2 + i % 2, 0:P], PT_[:, GT, tok(i)], ident)
                    tr(PS[:, 2 + i % 2, P:2 * P], g_m[:, tok(i)], ident).then_inc(gT.sem, 1)
                for q in range(4):
                    last = mm(PS[:, 4, NC * q:NC * q + NC], const(K_PAIR + q * P, P, 64), g_lf[0:64, C - 1::C],
                              start=True, stop=True)
                last.then_inc(gc_mm.sem, 1)
                pe.wait_ge(*ml_k.at(l, 2))

                def k_natural(u):
                    s, d = u // 2, u % 2
                    ch = ORDER[d][s]
                    if u >= 2:
                        pe.wait_ge(*kE_done.at(l, u - 1))
                    tr(PS[:, 5 + d, 0:P], PT_[:, MK, tok(ch)], ident)
                    tr(PS[:, 5 + d, P:2 * P], PT_[:, MK + 1, tok(ch)], ident).then_inc(kT.sem, 1)

                def key_value(u):
                    s, d = u // 2, u % 2
                    ch = ORDER[d][s]
                    pe.wait_ge(*kE_done.at(l, u + 1))
                    pe.wait_ge(*v1_done.at(l, NC))
                    if u >= 2:
                        pe.wait_ge(*cst_done.at(l, u - 1))
                    elif d == 1:
                        pe.wait_ge(*gc_done.at(l, 1))
                    bank = 7 if d == 0 else 4
                    for h in range(4):
                        pr = h % 2
                        w0 = (h // 2) * (HD + 1)
                        last = mm(PS[64 * pr:64 * pr + 64, bank, w0:w0 + HD + 1],
                                  kE[:, d, h * HD:h * HD + HD], V1[:, ch, h, :], start=True, stop=True)
                    last.then_inc(kv.sem, 1)

                k_natural(0)
                for u in range(10):
                    if u < 9:
                        k_natural(u + 1)
                    key_value(u)
                pe.wait_ge(*qz_done.at(l, 4))
                pe.wait_ge(*cst_done.at(l, 10))
                pe.wait_ge(*gcol_done.at(l, NC))

                def spread(g, bank, i, d):
                    row = g[0:64, tok(STEP[d][i])]
                    if d:
                        row = row[:, ::-1]
                    for h in range(4):
                        last = mm(PS[:, bank + d, h * C:h * C + C], const(K_SEL + (4 * d + h) * P, P, 64),
                                  row, start=True, stop=True)
                    return last

                def scores(r):
                    i = i0 + r
                    for d in range(2):
                        if r:
                            pe.wait_ge(*m_arg.at(l, 2 * r))
                        spread(g_b, 1, i, d).then_inc(m_a.sem, 1)
                    if r:
                        pe.wait_ge(*m_ds.at(l, 2 * r))
                    for h in range(4):
                        last = mm(PS[:, 0, h * C:h * C + C], PT_[:, MK + h // 2, tok(i)], qz[:, h, tok(i)],
                                  start=True, stop=True)
                    last.then_inc(m_scores.sem, 1)

                scores(0)
                for i in range(i0, NC):
                    r = i - i0
                    for d in range(2):
                        if r:
                            pe.wait_ge(*m_read.at(l, 2 * r))
                        spread(g_lf, 3, i, d).then_inc(m_g.sem, 1)
                    late_parts(2)
                    for d in range(2):
                        pe.wait_ge(*m_qg.at(l, 2 * r + d + 1))
                        pe.wait_ge(*m_ds.at(l, 2 * r + d + 1))
                        s = STEP[d][i]
                        for h in range(4):
                            o = PS[:, 3 + d, h * (HD + 1):(h + 1) * (HD + 1)]
                            last = mm(o, DD[r % 2][:, d, h * C:h * C + C], V1[:, i, h, :], start=True, stop=(s == 0))
                            if s:
                                last = mm(o, qG[d][:, h * C:h * C + C], Cst[d][:, h // 2, s, :], start=False, stop=True)
                        last.then_inc(m_num.sem, 1)
                    if i + 1 < NC:
                        scores(r + 1)
                    late_parts(2)
                    pe.wait_ge(*m_rows.at(l, r + 1))
                    if r:
                        pe.wait_ge(*m_out.at(l, r))
                    for t in range(2):
                        last = tr(PS[:, 5, t * P:t * P + P], HN[:, 0, t * P:t * P + P], ident)
                    last.then_inc(m_turned.sem, 1)

            def hgrn(l):
                i0 = 0 if l == 0 else 2
                late_finish()
                pe.wait_ge(*m_out.at(l, NC - i0))

                def scores(e):
                    pe.wait_ge(*h_copied.at(l, e + 1))
                    for half in range(2):
                        if e:
                            pe.wait_ge(*h_masked.at(l, 2 * e - 1 + half))
                        rows = slice(64 * half, 64 * half + 64)
                        for i in range(i0, NC):
                            for t in range(2):
                                t0 = t * T + i * C
                                col = (2 * (i % 2) + t) * C
                                last = mm(PS[:, 3 * half + i // 2, col:col + C], Kc[e % 2][rows, t0:t0 + C],
                                          Qc[e % 2][rows, t0:t0 + C], start=True, stop=True)
                        last.then_inc(h_scores.sem, 1)

                scores(0)
                scores(1)
                for i in range(NC):
                    if i >= 2:
                        pe.wait_ge(*vz_done.at(l, i - 1))
                    tr(PS[:, 6 + i % 2, 0:P], PT_[:, HV, tok(i)], ident)
                    tr(PS[:, 6 + i % 2, P:2 * P], PT_[:, HV + 1, tok(i)], ident).then_inc(hvT.sem, 1)
                for e in range(2, LEVELS + 1):
                    scores(e)
                    if e == 2:
                        pe.wait_ge(*vz_done.at(l, NC))
                    late_parts(2 if l == 0 else (2, 1, 1, 1, 1, 2)[e - 2])
                late_finish()
                pe.wait_ge(*h_updated.at(l, 7))
                pe.wait_ge(*h_masked.at(l, 16))

                def k_natural(u):
                    s, d = u // 2, u % 2
                    if u >= 2:
                        pe.wait_ge(*kn_done.at(l, u - 1))
                    t0 = ORDER[d][s] * C
                    tr(PS[:, d, 0:P], Kfb[:, d, t0:t0 + C], ident)
                    tr(PS[:, d, P:2 * P], Kfb[:, d, T + t0:T + t0 + C], ident).then_inc(hkT.sem, 1)

                def key_value(u):
                    s, d = u // 2, u % 2
                    pe.wait_ge(*kn_done.at(l, u + 1))
                    if u >= 2:
                        pe.wait_ge(*sst_done.at(l, u - 1))
                    for h in range(4):
                        pr = h % 2
                        last = mm(PS[:, 2 + d, h * HD:h * HD + HD], kn[:, d, h // 2, :],
                                  Vz[:, ORDER[d][s], h, 64 * pr:64 * pr + 64], start=True, stop=True)
                    last.then_inc(hkv.sem, 1)

                k_natural(0)
                for u in range(10):
                    if u < 9:
                        k_natural(u + 1)
                    key_value(u)
                pe.wait_ge(*sst_done.at(l, 10))
                for i in range(i0, NC):
                    for t in range(2):
                        o = PS[:, (4 + i) % 8, t * P:t * P + P]
                        first = True
                        for d in range(2):
                            s = STEP[d][i]
                            if s:
                                mm(o, Sst[:, d, t, s, :], Qfb[:, d, t * T + i * C:t * T + i * C + C], start=first,
                                   stop=False)
                                first = False
                        mm(o, Vz[:, i, 2 * t, :], A[:, 0, i, t, :], start=first, stop=False)
                        last = mm(o, Vz[:, i, 2 * t + 1, :], A[:, 1, i, t, :], start=False, stop=True)
                    last.then_inc(h_o.sem, 1)
                for t in range(2):
                    pe.wait_ge(*h_sq.at(l, t + 1))
                    for bank, (t0, tn) in enumerate(SEGS):
                        if l == 0 or bank:
                            last = mm(PS[:, 2 * t + bank, 0:tn], const(K_BLK, P), hsqr[:, t, t0:t0 + tn],
                                      start=True, stop=True)
                    last.then_inc(h_ms.sem, 1)

            def attention(l):
                pe.wait_ge(*hg_done.at(l, 1))
                for j in range(5):
                    if j >= 2:
                        pe.wait_ge(*a_rs.at(l, j - 1))
                    pe.wait_ge(*a_sq.at(l, j + 1))
                    for bank, (t0, tn) in enumerate(SEGS):
                        last = mm(PS[:, 2 * (j % 2) + bank, 0:tn], const(K_BLK, P), asq[:, j % 2, t0:t0 + tn],
                                  start=True, stop=True)
                    last.then_inc(a_ms.sem, 1)
                for j in range(5):
                    pe.wait_ge(*a_norm.at(l, j + 1))
                    if j >= 2:
                        pe.wait_ge(*a_sin.at(l, j - 1))
                    mm(PS[:, 4 + j % 2, :], const(K_ROT, P), PT_[:, AQ + j, CTX:T], start=True, stop=True)\
                        .then_inc(a_rot.sem, 1)
                for i in range(NC):
                    if i >= 2:
                        pe.wait_ge(*va_done.at(l, i - 1))
                    tr(PS[:, 6 + i % 2, 0:P], PT_[:, AV, tok(i)], ident).then_inc(avT.sem, 1)
                pe.wait_ge(*a_rope.at(l, 5))
                for q in range(4):
                    if q >= 2:
                        pe.wait_ge(*kz_done.at(l, q - 1))
                    elif q == 0:
                        pe.wait_ge(*a_rs.at(l, 5))
                    for bank, (t0, tn) in enumerate(SEGS):
                        last = mm(PS[:, 2 * (q % 2) + bank, 0:tn], const(K_KZ + q * P, P), PT_[:, AK, t0:t0 + tn],
                                  start=True, stop=True)
                    last.then_inc(kz_mm.sem, 1)
                pe.wait_ge(*kz_done.at(l, 4))
                units, prods = attn_units(l)

                def score(u):
                    h, q, nk, _ = units[u]
                    if u >= 2:
                        pe.wait_ge(*a_exp.at(l, u - 1))
                    lhs = PT_[:, AQ + h // 2, tok(q)]
                    kk = kz[:, 2 * (h // 4) + h % 2, :]
                    last = mm(PS[:, 2 * (u % 2), 0:min(nk, 4) * C], lhs, kk[:, 0:min(nk, 4) * C], start=True, stop=True)
                    if nk > 4:
                        last = mm(PS[:, 2 * (u % 2) + 1, 0:(nk - 4) * C], lhs, kk[:, 4 * C:nk * C], start=True, stop=True)
                    last.then_inc(a_s.sem, 1)

                def turn(u):
                    h, q, nk, pr = units[u]
                    pe.wait_ge(*a_scaled.at(l, u + 1))
                    if u:
                        pe.wait_ge(*turned_at(l, u - 1))
                    else:
                        pe.wait_ge(*a_sin.at(l, 5))
                    for kt in range(nk):
                        last = tr(PS[:, 4 + kt // 4, (kt % 4) * P:(kt % 4) * P + P], Pb[:, u % 2, tok(kt)], ident)
                    last.then_inc(a_T.sem, 1)

                def product(u):
                    h, q, nk, pr = units[u]
                    h, q0, nq, nk = prods[pr]
                    if q != q0 + nq - 1:
                        return
                    pe.wait_ge(*turned_at(l, u))
                    if u:
                        pe.wait_ge(*turned_at(l, u - 1))
                    pe.wait_ge(*va_done.at(l, NC))
                    if pr >= 2:
                        pe.wait_ge(*a_out.at(l, pr - 1))
                    r0, g0 = 64 * (h % 2), 64 * (h // 4)
                    for kt in range(nk):
                        last = mm(PS[r0:r0 + 64, 6 + pr % 2, 0:nq * C], Va[:, kt, g0:g0 + 64], PTr[:, pr % 2, kt, 0:nq * C],
                                  start=(kt == 0), stop=(kt == nk - 1))
                    last.then_inc(a_pv.sem, 1)

                score(0)
                score(1)
                for u in range(len(units)):
                    if u + 2 < len(units):
                        score(u + 2)
                    turn(u)
                    if u:
                        product(u - 1)
                product(len(units) - 1)

            for l in range(DEPTH):
                n_in, n_out, n_ff = slots(l)
                stats(l, 0, SEGS)
                for j in range(4):
                    free = evac_act.at(l, j - 1) if j >= 2 else (evac_dve.at(l, 0) if l else None)
                    gemm_slot(l, n_in + j, j, Uh, Ul, free, SEGS, (lambda k: u_ready.at(l, k + 1)) if j == 0 else None)
                pe.wait_ge(*wg_low.at(l, 1))
                for k in range(DK):
                    for bank, (t0, tn) in enumerate(SEGS):
                        o = PS[:, 6 + bank, 0:tn]
                        mm(o, wg_lo[:, k, :], Uh[:, k, t0:t0 + tn], start=(k == 0), stop=False)
                        mm(o, wg_hi[:, k, :], Ul[:, k, t0:t0 + tn], start=False, stop=False)
                        last = mm(o, wg_hi[:, k, :], Uh[:, k, t0:t0 + tn], start=False, stop=(k == DK - 1))
                last.then_inc(gate_mm.sem, 1)

                def project(i, ss):
                    for j in range(4):
                        gemm_slot(l, n_in + i * 4 + j, j, Uh, Ul, (evac_act.sem, 56 * l + i * 4 + j - 1), ss)

                if l == 0:
                    with pe.Fori(1, 6) as i:
                        project(i, SEGS)
                else:
                    project(1, segs(l))
                    with pe.Fori(2, 4) as i:
                        project(i, SEGS)
                    with pe.Fori(4, 6) as i:
                        project(i, segs(l))
                    pe.wait_ge(ctx_zero.sem, 5)
                mlstm(l)
                hgrn(l)
                attention(l)
                pe.wait_ge(*a_out.at(l, len(attn_units(l)[1])))
                for j in range(8):
                    gemm_slot(l, n_out + j, j, Uh, Ul, evac_dve.at(l, j - 1) if j >= 2 else None, segs(l),
                              (lambda k: u_ready.at(l, 9 + k)) if j == 0 else None)
                stats(l, 1, segs(l))

                def mlp(g, n0):
                    for j in range(8):
                        free = (evac_dve.sem, 40 * l + g * 8 + 7 + j) if j < 2 else \
                            (evac_act.sem, 56 * l + 24 + g * 8 + j - 1)
                        gemm_slot(l, n_ff + g * 16 + j, j, Uh, Ul, free, segs(l),
                                  (lambda k: u_ready.at(l, 17 + k)) if j == 0 else None)
                    for j in range(8):
                        free = (evac_act.sem, 56 * l + 24 + g * 8 + 7 + j) if j < 2 else \
                            (evac_dve.sem, 40 * l + 8 + g * 8 + j - 1)
                        gemm_slot(l, n_ff + g * 16 + 8 + j, j, hidh, hidl, free, segs(l),
                                  (lambda k: (hid_ready.sem, 32 * l + g * 8 + k + 1)) if j == 0 else None)

                with pe.Fori(0, FG) as g:
                    mlp(g, n_ff)
            for i in range(4):
                if i >= 2:
                    pe.wait_ge(out_act.sem, i - 1)
                    pe.wait_ge(out_dve.sem, i - 1)
                pe.wait_ge(*evac_dve.at(2, 0))
                for half in range(2):
                    for q in range(4):
                        last = tr(PS[:, 4 + 2 * (i % 2) + half, q * P:q * P + P], H[:, 4 * half + q, CTX + i * C:CTX + i * C + C],
                                  ident)
                    last.then_inc(out_T.sem, 1)

        @block.scalar
        def _(act):
            steps = [0]
            ac = nc.scalar.activation

            def own(ins):
                steps[0] += 1
                ins.then_inc(act_step.sem, 1)
                act.wait_ge(act_step.sem, steps[0])

            def split(n, j, wait_value):
                act.wait_ge(w_loaded[j % 4].sem, wait_value)
                act.wait_ge(gemm.sem, n - 1)
                ac(whi[:, j % 2, :, :], raw[:, j % 4, :, :], ACT.Copy).then_inc(w_high.sem, 1)

            def square(l, w, k):
                if k >= 2:
                    act.wait_ge(*n_sum.at(l, 8 * w + k - 1))
                t0 = segs(l)[0][0] if w else 0
                ac(sqb[:, k % 2, t0:T], H[:, k, t0:T], ACT.Square).then_inc(n_square.sem, 1)

            def inverse_rms(l, w, ss):
                act.wait_ge(*n_stat.at(l, w + 1))
                for bank, (t0, tn) in enumerate(SEGS):
                    if (t0, tn) in ss:
                        last = ac(rsb[:, t0:t0 + tn], PS[:, 4 + bank, 0:tn], ACT.Ln, bias=EPST[:, 0:1])
                own(last)
                ac(rsb[:, ss[0][0]:T], rsb[:, ss[0][0]:T], ACT.Exp, scale=-0.5).then_inc(n_rs.sem, 1)

            def u_high_part(l, w, ss):
                shift = 0 if w == 0 else 24
                for k in range(DK):
                    act.wait_ge(*n_scaled.at(l, 8 * w + k + 1))
                    for t0, tn in ss:
                        who = 1 if t0 == 0 else 0
                        last = ac(Uh[:, k, t0:t0 + tn], tb[:, k % 2, t0:t0 + tn], ACT.Identity,
                                  bias=MOD[:, l, shift + k, who:who + 1])
                    last.then_inc(u_high.sem, 1)

            nc.scalar.preload_act_table_set("natural_log_exp_and_others")

            def sigmoid(ap):
                own(ac(ap, ap, ACT.Exp, scale=-1.0))
                own(ac(ap, ap, ACT.Ln, bias=1.0))
                return ac(ap, ap, ACT.Exp, scale=-1.0)

            act.wait_ge(par_ready.sem, 1)
            ac(CS[:, :, :], V[:, V_C:V_C + 16].rearrange("p (w k) -> p k w", w=2), ACT.Exp, scale=-1.0)\
                .then_inc(c_exp.sem, 1)
            act.wait_ge(lb_max.sem, 1)
            ac(LBT[:, 1:3, :], LBT[:, 1:3, :], ACT.Exp).then_inc(lb_exp.sem, 1)
            for n in range(0, 12, 2):
                act.wait_ge(x_T.sem, n + 1)
                i, half = n // 2, n % 2
                ac(H[:, 4 * half:4 * half + 4, tok(i)], PS[:, 2 + n % 4, :].rearrange("p (k c) -> p k c", k=4),
                   ACT.Copy).then_inc(x_act.sem, 1)
            for s in range(EARLY):
                act.wait_ge(mod_mm.sem, s + 1)
                ac(modrow[0:2, 512 * s:512 * s + 512], PS[0:2, 6 + s % 2, :], ACT.Copy)\
                    .then_inc(mod_row.sem, 1)

            rows_taken = [0, 0]

            def late_columns():
                g = rows_taken[1]
                layer, group = divmod(EARLY + g, MOD_GROUPS // 2)
                act.wait_ge(late_turned.sem, g + 1)
                ac(MOD[:, layer, 4 * group:4 * group + 4, :], PS[:, 7, 0:8].rearrange("p (m w) -> p m w", w=2),
                   ACT.Copy).then_inc(late_taken.sem, 1)
                rows_taken[1] += 1

            def late_rows(n=1, finish=False):
                for _ in range(n):
                    g = rows_taken[0]
                    if rows_taken[1] < g:
                        late_columns()
                    act.wait_ge(late_part.sem, 4 * g + 4)
                    ac(late_row_buf[:, :], PS[0:2, 6, :], ACT.Copy).then_inc(late_row.sem, 1)
                    rows_taken[0] += 1
                if finish:
                    late_columns()

            def mlstm(l):
                i0 = 0 if l == 0 else 2
                own(ac(g_lf[64:P, :], PT_[64:P, GT, :], ACT.Abs))
                own(ac(g_lf[64:P, :], g_lf[64:P, :], ACT.Exp, scale=-1.0))
                ac(g_lf[64:P, :], g_lf[64:P, :], ACT.Ln, bias=1.0).then_inc(g_softplus.sem, 1)
                for i in range(NC):
                    act.wait_ge(*vT.at(l, i + 1))
                    if i == 0:
                        act.wait_ge(*v1_ones.at(l, 1))
                    ac(V1[:, i, :, 0:HD], PS[:, i % 2, 0:256].rearrange("p (h e) -> p h e", h=4), ACT.Copy)\
                        .then_inc(v1_done.sem, 1)
                for j in range(2):
                    act.wait_ge(*ml_q.at(l, j + 1))
                    for pr in range(2):
                        ac(qz[:, 2 * j + pr, :], PT_[:, MQ + j, :], ACT.Copy, scale=const(K_HM + pr, 1))\
                            .then_inc(qz_done.sem, 1)
                act.wait_ge(*g_rows.at(l, 1))
                ac(g_lf[0:64, :], g_lf[0:64, :], ACT.Exp)
                ac(PT_[0:32, GT, :], g_ig[0:32, :], ACT.Copy)
                ac(PT_[64:96, GT, :], g_e[0:32, :], ACT.Exp)
                ac(g_m[64:96, :], g_m[0:32, :], ACT.Exp)
                for t0, tn in SEGS:
                    ac(PT_[32:64, GT, t0:t0 + tn], g_ig[32:64, t0:t0 + tn][:, ::-1], ACT.Copy)
                    ac(g_m[96:P, t0:t0 + tn], g_m[32:64, t0:t0 + tn][:, ::-1], ACT.Exp)
                    last = ac(PT_[96:P, GT, t0:t0 + tn], g_e[32:64, t0:t0 + tn][:, ::-1], ACT.Exp)
                last.then_inc(g_exp.sem, 1)
                late_rows(LATE_FIRST[l], finish=True)
                for i in range(NC):
                    act.wait_ge(*gT.at(l, i + 1))
                    src = PS[:, 2 + i % 2, 0:2 * P].rearrange("p (n d c) -> p n d c", n=4, d=2)
                    ac(GCOL[:, i, 0:2, :, :], src[:, 0:2, :, 0:4], ACT.Copy)
                    ac(GCOL[:, i, 2, :, :], src[:, 3, :, 0:4], ACT.Copy).then_inc(gcol_done.sem, 1)
                for r in range(NC - i0):
                    for d in range(2):
                        act.wait_ge(*m_arg.at(l, 2 * r + d + 1))
                        ac(DD[r % 2][:, d, :], DD[r % 2][:, d, :], ACT.Exp).then_inc(m_dexp.sem, 1)
                    if r:
                        late_rows()

            def hgrn(l):
                i0 = 0 if l == 0 else 2
                late_rows(finish=True)
                act.wait_ge(*h_f.at(l, 1))
                ac(Qc[0][:, :], PT_[:, HQ:HQ + 2, :].rearrange("p t n -> p (t n)"), ACT.Copy).then_inc(h_copied.sem, 1)

                def values():
                    act.wait_ge(*vz_zero.at(l, 1))
                    for i in range(NC):
                        act.wait_ge(*hvT.at(l, i + 1))
                        src = PS[:, 6 + i % 2, 0:256].rearrange("p (h e) -> p h e", h=4)
                        for pr in range(2):
                            last = ac(Vz[:, i, pr::2, 64 * pr:64 * pr + 64], src[:, pr::2, :], ACT.Copy)
                        last.then_inc(vz_done.sem, 1)

                for lv in range(LEVELS):
                    if lv == 2:
                        values()
                    b = 1 << lv

                    def halves(ap):
                        return ap.rearrange("p (n two b) -> p n two b", two=2, b=b)

                    if lv:
                        act.wait_ge(*h_updated.at(l, lv))
                    q_l, k_l = Qc[(lv + 1) % 2], Kc[(lv + 1) % 2]
                    if lv:
                        act.wait_ge(*h_scores.at(l, 2 * lv))
                    else:
                        act.wait_ge(*h_copied.at(l, 1))
                    if lv in ((4, 6) if l == 0 else (5,)):
                        late_rows()
                    for side, d in ((1, 0), (0, 1)):
                        ac(halves(q_l[:, :])[:, :, side, :], halves(Qfb[:, d, :])[:, :, side, :], ACT.Copy)
                    ac(halves(k_l[:, :])[:, :, 0, :], halves(Kfb[:, 0, :])[:, :, 0, :], ACT.Copy)
                    ac(halves(k_l[:, :])[:, :, 1, :], halves(Kfb[:, 1, :])[:, :, 1, :], ACT.Copy)\
                        .then_inc(h_copied.sem, 1)
                late_rows(finish=True)
                act.wait_ge(*h_scores.at(l, 16))
                for u in range(10):
                    act.wait_ge(*hkT.at(l, u + 1))
                    if u >= 2:
                        act.wait_ge(*hkv.at(l, u - 1))
                    ac(kn[:, u % 2, :, :], PS[:, u % 2, 0:256].rearrange("p (t c) -> p t c", t=2), ACT.Copy)\
                        .then_inc(kn_done.sem, 1)
                for i in range(i0, NC):
                    act.wait_ge(*h_o.at(l, i - i0 + 1))
                    last = ac(PT_[:, HQ:HQ + 2, tok(i)],
                              PS[:, (4 + i) % 8, 0:256].rearrange("p (t c) -> p t c", t=2),
                              ACT.Copy)
                    last.then_inc(h_oe.sem, 1)
                act.wait_ge(*h_oe.at(l, NC - i0))
                t0 = i0 * C
                for t in range(2):
                    ac(hsqr[:, t, t0:T], PT_[:, HQ + t, t0:T], ACT.Square).then_inc(h_sq.sem, 1)
                act.wait_ge(*g_clamped.at(l, 1))
                sigmoid(hsg[:, :, :]).then_inc(g_silu_exp.sem, 1)
                for t in range(2):
                    act.wait_ge(*h_ms.at(l, t + 1))
                    for bank, (a0, an) in enumerate(SEGS):
                        if a0 >= t0:
                            last = ac(hrs[:, t, a0:a0 + an], PS[:, 2 * t + bank, 0:an], ACT.Ln, bias=EPST[:, 0:1])
                    own(last)
                    ac(hrs[:, t, t0:T], hrs[:, t, t0:T], ACT.Exp, scale=-0.5).then_inc(h_rs.sem, 1)

            def attention(l):
                act.wait_ge(*hg_done.at(l, 1))

                def square(j):
                    if j >= 2:
                        act.wait_ge(*a_ms.at(l, j - 1))
                    ac(asq[:, j % 2, :], PT_[:, AQ + j, :], ACT.Square).then_inc(a_sq.sem, 1)

                square(0)
                for j in range(5):
                    if j < 4:
                        square(j + 1)
                    act.wait_ge(*a_ms.at(l, j + 1))
                    if j >= 2:
                        act.wait_ge(*a_norm.at(l, j - 1))
                    for bank, (t0, tn) in enumerate(SEGS):
                        last = ac(ars[:, j % 2, t0:t0 + tn], PS[:, 2 * (j % 2) + bank, 0:tn], ACT.Ln,
                                  bias=EPST[:, 0:1])
                    own(last)
                    ac(ars[:, j % 2, :], ars[:, j % 2, :], ACT.Exp, scale=-0.5).then_inc(a_rs.sem, 1)
                for i in range(NC):
                    act.wait_ge(*avT.at(l, i + 1))
                    ac(Va[:, i, :], PS[:, 6 + i % 2, 0:P], ACT.Copy)\
                        .then_inc(va_done.sem, 1)
                for q in range(4):
                    act.wait_ge(*kz_mm.at(l, q + 1))
                    for bank, (t0, tn) in enumerate(SEGS):
                        last = ac(kz[:, q, t0:t0 + tn], PS[:, 2 * (q % 2) + bank, 0:tn], ACT.Copy)
                    last.then_inc(kz_done.sem, 1)
                units, prods = attn_units(l)

                def probs(u):
                    h, q, nk, _ = units[u]
                    act.wait_ge(*a_max.at(l, u + 1))
                    if u >= 2:
                        act.wait_ge(*a_T.at(l, u - 1))
                    src = PS[:, 2 * (u % 2):2 * (u % 2) + 2, :].rearrange("p b n -> p (b n)")[:, 0:nk * C]
                    ac(Pb[:, u % 2, 0:nk * C], src, ACT.Exp, bias=NEGM[:, u % 2:u % 2 + 1],
                       accum_out=PSUMS[:, u % 2:u % 2 + 1]).then_inc(a_exp.sem, 1)

                def turned(u):
                    h, q, nk, pr = units[u]
                    q0 = prods[pr][1]
                    if u % 2:
                        return
                    act.wait_ge(*a_T.at(l, u + 1))
                    if pr >= 2:
                        act.wait_ge(*a_pv.at(l, pr - 1))
                    src = PS[:, 4:6, :].rearrange("p b n -> p (b n)")[:, 0:nk * C]
                    ac(PTr[:, pr % 2, 0:nk, (q - q0) * C:(q - q0) * C + C],
                       src.rearrange("p (k c) -> p k c", k=nk), ACT.Copy).then_inc(a_Tact.sem, 1)

                def take(u):
                    h, q, nk, pr = units[u]
                    _, q0, nq, _ = prods[pr]
                    if q != q0 + nq - 1:
                        return
                    act.wait_ge(*a_pv.at(l, pr + 1))
                    r0 = 64 * (h % 2)
                    ac(AO[r0:r0 + 64, h // 2, q0 * C:(q0 + nq) * C], PS[r0:r0 + 64, 6 + pr % 2, 0:nq * C], ACT.Copy)\
                        .then_inc(a_out.sem, 1)

                probs(0)
                for u in range(len(units)):
                    if u:
                        turned(u - 1)
                    if u + 1 < len(units):
                        probs(u + 1)
                    if u >= 2:
                        take(u - 2)
                turned(len(units) - 1)
                take(len(units) - 2)
                take(len(units) - 1)

            act.wait_ge(mod_ready.sem, 1)
            for l in range(DEPTH):
                n_in, n_out, n_ff = slots(l)
                act.wait_ge(x_dve.sem, 6)
                act.wait_ge(x_act.sem, 6)
                if l == 0:
                    act.wait_ge(w_loaded[0].sem, 16)
                    ac(whi[:, 0, :, :], raw[:, 0, :, :], ACT.Copy).then_inc(w_high.sem, 1)
                if l == 0:
                    act.wait_ge(*wg_loaded.at(l, 64))
                    ac(wg_hi[:, :, :], wg_raw[:, :, :], ACT.Copy).then_inc(wg_high.sem, 1)
                if l == 0:
                    for k in range(DK):
                        square(0, 0, k)
                inverse_rms(l, 0, SEGS)
                u_high_part(l, 0, SEGS)
                if l:
                    act.wait_ge(*wg_loaded.at(l, 64))
                    ac(wg_hi[:, :, :], wg_raw[:, :, :], ACT.Copy).then_inc(wg_high.sem, 1)
                def take_gates():
                    act.wait_ge(*gate_mm.at(l, 1))
                    act.wait_ge(gate_bias_zero.sem, 128)
                    for bank, (t0, tn) in enumerate(SEGS):
                        last = ac(PT_[:, GT, t0:t0 + tn], PS[:, 6 + bank, 0:tn], ACT.Identity, bias=GB[:, l:l + 1])
                    last.then_inc(gate_tok.sem, 1)

                def beside(s):
                    if s == 4:
                        take_gates()
                    if 9 <= s < 13:
                        j = s - 9
                        act.wait_ge(*conv_done.at(l, j + 1))
                        sigmoid(PT_[:, MQ + j, :]).then_inc(ml_exp.sem, 1)
                    if 13 <= s < 15:
                        if s == 13:
                            act.wait_ge(*o_clamped.at(l, 1))
                        sigmoid(PT_[:, MO + s - 13, :]).then_inc(o_exp.sem, 1)
                    if 16 <= s < 20:
                        if s == 16:
                            act.wait_ge(*z_clamped.at(l, 1))
                        sigmoid(PT_[:, HZ + s - 16, :]).then_inc(z_exp.sem, 1)

                for s in range(IN_TILES):
                    n, m = n_in + s, IN_ORDER[s]
                    split(n + 1, s + 1, (n + 1) // 4 * 16 + 16)
                    if s == 20:
                        act.wait_ge(*ml_q.at(l, 2))
                        act.wait_ge(*ml_k.at(l, 2))
                    act.wait_ge(gemm.sem, n + 1)
                    for bank, (t0, tn) in enumerate(SEGS):
                        if l == 0 or bank or s // 4 not in LAT_GROUPS:
                            last = ac(PT_[:, m, t0:t0 + tn], PS[:, 2 * (s % 2) + bank, 0:tn], ACT.Identity,
                                      bias=par(V_BIN + 24 * l + m))
                    last.then_inc(evac_act.sem, 1)
                    beside(s)
                act.wait_ge(*evac_act.at(l, 24))
                if l:
                    act.wait_ge(ctx_zero.sem, 5)
                act.wait_ge(*gate_tok.at(l, 1))
                mlstm(l)
                hgrn(l)
                attention(l)
                s0 = segs(l)[0][0]
                act.wait_ge(*a_out.at(l, len(attn_units(l)[1])))
                for k in range(DK):
                    src = AO[:, k, s0:T] if k < 4 else PT_[:, (HQ if k < 6 else MO) + k % 2, s0:T]
                    ac(Uh[:, k, s0:T], src, ACT.Copy).then_inc(u_high.sem, 1)
                for j in range(9):
                    n = n_out + j
                    if j < 8:
                        split(n + 1, j + 1, (n + 1) // 4 * 16 + 16)
                    if j:
                        act.wait_ge(*evac_dve.at(l, j))
                        square(l, 1, j - 1)
                inverse_rms(l, 1, segs(l))
                act.wait_ge(late_ready.sem, l + 1)
                u_high_part(l, 1, segs(l))

                def mlp(g, last_group=False):
                    for j in range(8):
                        n = n_ff + g * 16 + j
                        split(n + 1, j + 1, (n_ff // 4 + g * 4 + (j + 1) // 4 + 1) * 16)
                        act.wait_ge(gemm.sem, n + 1)
                        f = 32 * l + g * 8 + j
                        if not isinstance(f, int) or f >= 2:
                            act.wait_ge(hid_ready.sem, f - 1)
                        for bank, (t0, tn) in enumerate(SEGS):
                            if (t0, tn) in segs(l):
                                last = ac(relu[:, j % 2, t0:t0 + tn], PS[:, 2 * (j % 2) + bank, 0:tn], ACT.Relu)
                        last.then_inc(evac_act.sem, 1)
                        act.wait_ge(evac_act.sem, 56 * l + 24 + g * 8 + j + 1)
                        t0 = segs(l)[0][0]
                        ac(hidh[:, j, t0:T], relu[:, j % 2, t0:T], ACT.Square).then_inc(hid_high.sem, 1)
                    for j in range(9):
                        n = n_ff + g * 16 + 8 + j
                        if j < (7 if last_group and l else 8):
                            split(n + 1, j + 1, (n_ff // 4 + g * 4 + 2 + (j + 1) // 4 + 1) * 16)
                        if j and last_group and l == 0:
                            act.wait_ge(*evac_dve.at(l, 32 + j))
                            square(l + 1, 0, j - 1)

                mlp(0)
                with act.Fori(1, FG - 1) as g:
                    mlp(g)
                mlp(FG - 1, True)
            for i in range(4):
                act.wait_ge(out_T.sem, 2 * i + 1)
                ac(onat[:, i, 0:512], PS[:, 4 + 2 * (i % 2), :], ACT.Copy).then_inc(out_act.sem, 1)

        @block.vector
        def _(dve):
            steps = [0]
            tt, ts, stt, cp = nc.vector.tensor_tensor, nc.vector.tensor_scalar, nc.vector.scalar_tensor_tensor, \
                nc.vector.tensor_copy

            def own(ins):
                steps[0] += 1
                ins.then_inc(dve_step.sem, 1)
                dve.wait_ge(dve_step.sem, steps[0])

            def low(n, j):
                dve.wait_ge(w_high.sem, n + 1)
                tt(wlo[:, j % 2, :, :], raw[:, j % 4, :, :], whi[:, j % 2, :, :].bitcast(F32), ALU.subtract)\
                    .then_inc(w_low.sem, 1)

            def sum_square(l, w, k):
                dve.wait_ge(*n_square.at(l, 8 * w + k + 1))
                t0 = segs(l)[0][0] if w else 0
                if k == 0:
                    cp(rsb[:, t0:T], sqb[:, 0, t0:T]).then_inc(n_sum.sem, 1)
                else:
                    dve.wait_ge(*n_sum.at(l, 8 * w + k))
                    tt(rsb[:, t0:T], rsb[:, t0:T], sqb[:, k % 2, t0:T], ALU.add).then_inc(n_sum.sem, 1)

            def u_parts(l, w, ss):
                dve.wait_ge(*n_rs.at(l, w + 1))
                shift = 0 if w == 0 else 24
                for k in range(DK + 1):
                    if k < DK:
                        if k >= 2:
                            dve.wait_ge(*u_high.at(l, 16 * w + k - 1))
                            dve.wait_ge(*u_ready.at(l, 16 * w + k - 1))
                        for t0, tn in ss:
                            who = 1 if t0 == 0 else 0
                            last = stt(tb[:, k % 2, t0:t0 + tn], H[:, k, t0:t0 + tn], GAIN[:, l, w, k, who:who + 1],
                                       rsb[:, t0:t0 + tn], ALU.mult, ALU.mult)
                        last.then_inc(n_scaled.sem, 1)
                    if k:
                        dve.wait_ge(*u_high.at(l, 16 * w + k))
                        dve.wait_ge(*n_scaled.at(l, 8 * w + k))
                        for t0, tn in ss:
                            who = 1 if t0 == 0 else 0
                            last = stt(Ul[:, k - 1, t0:t0 + tn], tb[:, (k - 1) % 2, t0:t0 + tn],
                                       MOD[:, l, shift + k - 1, who:who + 1], Uh[:, k - 1, t0:t0 + tn].bitcast(F32),
                                       ALU.add, ALU.subtract)
                        last.then_inc(u_ready.sem, 1)

            dve.wait_ge(par_T.sem, 1)
            dve.wait_ge(const_loaded.sem, 17 * 16)
            own(cp(M8[:, :, :], mask_in[:, :, :]))
            dve.memset(EPST[:, :], EPS)
            cp(V[:, :], PS[:, 0, 0:V_N]).then_inc(par_ready.sem, 1)
            dve.wait_ge(par_ready.sem, 1)
            a0, a1 = V[:, V_LB:V_LB + 4], V[:, V_LB + 4:V_LB + 8]
            own(tt(LBT[:, 0, :], a0, a1, ALU.max))
            tt(LBT[:, 1, :], a0, LBT[:, 0, :], ALU.subtract)
            tt(LBT[:, 2, :], a1, LBT[:, 0, :], ALU.subtract).then_inc(lb_max.sem, 1)
            dve.wait_ge(c_exp.sem, 1)
            own(ts(CS[:, :, :], CS[:, :, :], 1.0, None, ALU.add))
            own(nc.vector.reciprocal(CS[:, :, :], CS[:, :, :]))
            tt(CS[:, :, :], CS[:, :, :], V[:, V_C:V_C + 16].rearrange("p (w k) -> p k w", w=2), ALU.mult)\
                .then_inc(c_silu.sem, 1)
            dve.wait_ge(lb_exp.sem, 1)
            own(tt(LBT[:, 3, :], LBT[:, 1, :], LBT[:, 2, :], ALU.add))
            own(nc.vector.reciprocal(LBT[:, 4, :], LBT[:, 3, :]))
            dve.memset(LB[:, 0, :], 0.0)
            dve.memset(LB1[:, 0, :], 1.0)
            own(tt(LB[:, 1, :], LBT[:, 2, :], LBT[:, 4, :], ALU.mult))
            own(ts(LB1[:, 1, :], LB[:, 1, :], -1.0, 1.0, ALU.mult, ALU.add))
            own(ts(V[:, V_QN:V_QN + 2], V[:, V_QN:V_QN + 2], HD ** -0.5, None, ALU.mult))
            for n in range(1, 12, 2):
                dve.wait_ge(x_T.sem, n + 1)
                i, half = n // 2, n % 2
                cp(H[:, 4 * half:4 * half + 4, tok(i)], PS[:, 2 + n % 4, :].rearrange("p (k c) -> p k c", k=4))\
                    .then_inc(x_dve.sem, 1)

            def gains(layer, w):
                row, g = ((8, V_NMIX), (32, V_NFFN))[w]
                return stt(GAIN[:, layer, w, :, :], MOD[:, layer, row:row + 8, :], 1.0,
                           V[:, g + 8 * layer:g + 8 * layer + 8].unsqueeze(2).broadcast_to([P, DK, 2]), ALU.add, ALU.mult)

            dve.wait_ge(mod_T.sem, 1)
            own(tt(MOD[:, 0, 0:4 * EARLY, :], PS[:, 1, 0:8 * EARLY].rearrange("p (m w) -> p m w", w=2),
                   V[:, V_BMOD:V_BMOD + 4 * EARLY].unsqueeze(2).broadcast_to([P, 4 * EARLY, 2]), ALU.add))
            own(gains(0, 0))
            dve.memset(EPST[:, 1:2], 0.0).then_inc(mod_ready.sem, 1)

            def mlstm(l):
                i0 = 0 if l == 0 else 2
                dve.wait_ge(*evac_act.at(l, 24))
                if l:
                    dve.wait_ge(ctx_zero.sem, 5)

                dve.wait_ge(*g_softplus.at(l, 1))
                own(stt(g_lf[64:P, :], PT_[64:P, GT, :], 0.0, g_lf[64:P, :], ALU.min, ALU.subtract))
                cp(g_lf[0:32, :], g_lf[64:96, :])
                cp(g_ig[0:32, :], PT_[0:32, GT, :])
                for a, n in SEGS:
                    cp(g_lf[32:64, a:a + n], g_lf[96:128, a:a + n][:, ::-1])
                    cp(g_ig[32:64, a:a + n], PT_[32:64, GT, a:a + n][:, ::-1])
                own(dve.memset(resets[:, :], 1.0))
                own(dve.memset(resets[:, 0:T:C], 0.0))
                dve.wait_ge(*ml_k.at(l, 2))
                nc.vector.tensor_tensor_scan(g_m[0:64, :], g_lf[0:64, :], g_ig[:, :], 0.0, ALU.add, ALU.max)
                own(nc.vector.tensor_tensor_scan(g_b[:, :], resets[:, :], g_lf[0:64, :], 0.0, ALU.mult, ALU.add))
                dve.memset(MPREV[:, 0:1], 0.0)
                cp(MPREV[:, 1:NC], g_m[0:64, C - 1:T - 1:C])
                own(tt(g_ig[:, :], g_ig[:, :], g_b[:, :], ALU.subtract))
                own(tt(g_b[:, :], g_b[:, :], g_m[0:64, :], ALU.subtract))

                def chunks(ap):
                    return ap.rearrange("p (i c) -> p i c", c=C)

                tt(chunks(g_lf[0:64, :]), chunks(g_b[:, :]), MPREV[:, :].unsqueeze(2).broadcast_to([64, NC, C]), ALU.add)
                ts(g_m[0:64, :], g_m[0:64, :], -1.0, 88.0, ALU.mult, ALU.min)
                tt(chunks(g_e[:, :]), chunks(g_ig[:, :]), g_b[:, C - 1::C].unsqueeze(2).broadcast_to([64, NC, C]),
                   ALU.add).then_inc(g_rows.sem, 1)
                dve.wait_ge(*gc_mm.at(l, 1))
                cp(GC[:, :, :], PS[:, 4, 0:4 * NC].rearrange("p (q s) -> p q s", q=4)).then_inc(gc_done.sem, 1)
                dve.wait_ge(*v1_done.at(l, NC))
                dve.wait_ge(*qz_done.at(l, 4))
                for d in range(2):
                    last = dve.memset(Cst[d][:, :, 0, :], 0.0)
                own(last)
                dve.wait_ge(*gcol_done.at(l, NC))

                def decayed_keys(u):
                    s, d = u // 2, u % 2
                    ch = ORDER[d][s]
                    dve.wait_ge(*kT.at(l, u + 1))
                    if u >= 2:
                        dve.wait_ge(*kv.at(l, u - 1))
                    tt(kE[:, d, :].rearrange("p (h e) -> p h e", h=4), PS[:, 5 + d, 0:256].rearrange("p (h e) -> p h e", h=4),
                       GCOL[:, ch, 1, d, :].unsqueeze(2).broadcast_to([P, 4, HD]), ALU.mult).then_inc(kE_done.sem, 1)

                def states(u):
                    s, d = u // 2, u % 2
                    dve.wait_ge(*kv.at(l, u + 1))
                    if u >= 2:
                        dve.wait_ge(*cst_done.at(l, u - 1))
                    for t in range(2):
                        last = stt(Cst[d][:, t, s + 1, :], Cst[d][:, t, s, :], GC[:, 2 * d + t, s:s + 1],
                                   PS[:, 7 if d == 0 else 4, t * (HD + 1):(t + 1) * (HD + 1)], ALU.mult, ALU.add)
                    last.then_inc(cst_done.sem, 1)

                dve.wait_ge(*gc_done.at(l, 1))
                decayed_keys(0)
                for u in range(10):
                    if u < 9:
                        decayed_keys(u + 1)
                    states(u)
                dve.wait_ge(*o_exp.at(l, 2))
                dve.wait_ge(*cst_done.at(l, 10))

                def arguments(r):
                    i = i0 + r
                    for d in range(2):
                        dve.wait_ge(*m_a.at(l, 2 * r + d + 1))
                        if r >= 2:
                            dve.wait_ge(*m_num.at(l, 2 * (r - 1)))
                        for h in range(4):
                            last = stt(DD[r % 2][:, d, h * C:h * C + C], PS[:, 1 + d, h * C:h * C + C],
                                       GCOL[:, i, 0, d, h:h + 1], const(K_MASK + d * C, C), ALU.add, ALU.add)
                        last.then_inc(m_arg.sem, 1)

                arguments(0)
                for i in range(i0, NC):
                    r = i - i0
                    for d in range(2):
                        dve.wait_ge(*m_g.at(l, 2 * r + d + 1))
                        if r:
                            dve.wait_ge(*m_num.at(l, 2 * r))
                        tt(qG[d][:, :].rearrange("p (h c) -> p h c", h=4), qz[:, :, tok(i)],
                           PS[:, 3 + d, :].rearrange("p (h c) -> p h c", h=4), ALU.mult).then_inc(m_qg.sem, 1)
                    dve.wait_ge(*m_scores.at(l, r + 1))
                    for d in range(2):
                        dve.wait_ge(*m_dexp.at(l, 2 * r + d + 1))
                        tt(DD[r % 2][:, d, :], PS[:, 0, :], DD[r % 2][:, d, :], ALU.mult).then_inc(m_ds.sem, 1)
                    if i + 1 < NC:
                        arguments(r + 1)
                    dve.wait_ge(*m_num.at(l, 2 * r + 2))
                    num = PS[:, 3:5, 0:4 * (HD + 1)].rearrange("p d (h e) -> p d h e", h=4)
                    own(tt(DEN[:, 0, :, :], num[:, :, :, HD:HD + 1].squeeze(3), GCOL[:, i, 2, :, :], ALU.max))
                    own(stt(DEN[:, 1, :, :], num[:, :, :, HD:HD + 1].squeeze(3), -1.0, DEN[:, 0, :, :], ALU.mult, ALU.max))
                    own(nc.vector.reciprocal(DEN[:, 1, :, :], DEN[:, 1, :, :]))
                    if r:
                        dve.wait_ge(*m_turned.at(l, r))
                    for d in range(2):
                        tt(HN[:, d, :].rearrange("p (h e) -> p h e", h=4), num[:, d, :, 0:HD],
                           DEN[:, 1, d, :].unsqueeze(2).broadcast_to([P, 4, HD]), ALU.mult).then_inc(m_read.sem, 1)
                    dve.wait_ge(*m_read.at(l, 2 * r + 2))
                    tt(HN[:, 0, :], HN[:, 0, :], HN[:, 1, :], ALU.add).then_inc(m_rows.sem, 1)
                    dve.wait_ge(*m_turned.at(l, r + 1))
                    tt(PT_[:, MO:MO + 2, tok(i)], PS[:, 5, 0:256].rearrange("p (t c) -> p t c", t=2),
                       PT_[:, MO:MO + 2, tok(i)], ALU.mult).then_inc(m_out.sem, 1)
                dve.wait_ge(*m_out.at(l, NC - i0))

            def hgrn(l):
                i0 = 0 if l == 0 else 2
                f = pyramid[0]
                dve.wait_ge(*forget.at(l, 4))
                own(ts(Kfb[:, :, :].rearrange("p d n -> p (d n)"), f[:, :], -1.0, 1.0, ALU.mult, ALU.add))
                q2 = PT_[:, HQ:HQ + 2, :].rearrange("p t n -> p (t n)")
                for d in range(2):
                    tt(Qfb[:, d, :], q2, f[:, 2 * d * T:2 * d * T + 2 * T], ALU.mult)
                tt(Kc[0][:, :], Kfb[:, 0, :], Kfb[:, 1, :], ALU.add).then_inc(h_f.sem, 1)
                dve.wait_ge(*h_f.at(l, 1))

                def masked(e):
                    for r in range(2):
                        dve.wait_ge(*h_scores.at(l, 2 * e + r + 1))
                        dst = A[:, r, i0:NC, :, :].rearrange("p i t c -> p (i t) c")
                        src = PS[:, 3 * r:3 * r + 3, :].rearrange("p b (n c) -> p (b n) c", c=C)[:, 2 * i0:2 * NC, :]
                        nc.vector.copy_predicated(dst, M8[:, e, :].unsqueeze(1).broadcast_to([P, 2 * (NC - i0), C]), src)\
                            .then_inc(h_masked.sem, 1)

                masked(0)
                for lv in range(LEVELS):
                    b = 1 << lv
                    dve.wait_ge(*h_copied.at(l, lv + 2))
                    if lv:
                        dve.wait_ge(*h_updated.at(l, lv))

                    def halves(ap, side):
                        return ap.rearrange("p (n two b) -> p n two b", two=2, b=b)[:, :, side, :]

                    nb = T // b

                    def total(d, side):
                        p_ = pyramid[lv][:, d * (2 * T >> lv):(d + 1) * (2 * T >> lv)]
                        return p_.rearrange("p (n two) -> p n two", two=2)[:, :, side:side + 1].broadcast_to([P, nb, b])

                    for arr, d, side in ((Qfb, 0, 1), (Qfb, 1, 0), (Kfb, 0, 0), (Kfb, 1, 1)):
                        tt(halves(arr[:, d, :], side), halves(arr[:, d, :], side), total(d, 1 - side), ALU.mult)
                    pair = pyramid[lv][:, :].rearrange("p (n two) -> p n two", two=2)
                    tt(pyramid[lv + 1][:, :], pair[:, :, 0], pair[:, :, 1], ALU.mult).then_inc(h_updated.sem, 1)
                    masked(lv + 1)
                dve.wait_ge(*h_updated.at(l, 7))
                dve.wait_ge(*sst_zero.at(l, 1))
                T7 = pyramid[LEVELS]
                for u in range(10):
                    s, d = u // 2, u % 2
                    dve.wait_ge(*hkv.at(l, u + 1))
                    if u >= 2:
                        dve.wait_ge(*sst_done.at(l, u - 1))
                    for t in range(2):
                        for pr in range(2):
                            rows = slice(64 * pr, 64 * pr + 64)
                            col = (2 * d + t) * NC + ORDER[d][s]
                            last = stt(Sst[rows, d, t, s + 1, 64 * pr:64 * pr + 64], Sst[rows, d, t, s, 64 * pr:64 * pr + 64],
                                       T7[rows, col:col + 1], PS[rows, 2 + d, t * P + 64 * pr:t * P + 64 * pr + 64],
                                       ALU.mult, ALU.add)
                    last.then_inc(sst_done.sem, 1)
                dve.wait_ge(*hkT.at(l, 10))
                ts(hsg[:, :, :], PT_[:, HG:HG + 2, :], -41.0, None, ALU.max).then_inc(g_clamped.sem, 1)
                dve.wait_ge(*g_silu_exp.at(l, 1))
                tt(hsg[:, :, :], hsg[:, :, :], PT_[:, HG:HG + 2, :], ALU.mult)
                t0 = i0 * C
                dve.wait_ge(*h_rs.at(l, 2))
                for t in range(2):
                    last = stt(PT_[:, HQ + t, t0:T], PT_[:, HQ + t, t0:T], par(V_HN + l), hrs[:, t, t0:T], ALU.mult,
                               ALU.mult)
                own(last)
                tt(PT_[:, HQ:HQ + 2, t0:T], PT_[:, HQ:HQ + 2, t0:T], hsg[:, :, t0:T], ALU.mult).then_inc(hg_done.sem, 1)

            def attention(l):
                for j in range(5):
                    dve.wait_ge(*a_rs.at(l, j + 1))
                    g = par((V_QN if j < 4 else V_KN) + l)
                    stt(PT_[:, AQ + j, :], PT_[:, AQ + j, :], g, ars[:, j % 2, :], ALU.mult, ALU.mult)\
                        .then_inc(a_norm.sem, 1)
                for j in range(5):
                    dve.wait_ge(*a_rot.at(l, j + 1))
                    tt(rt[:, j % 2, :], PS[:, 4 + j % 2, :], const(K_SIN, LAT), ALU.mult).then_inc(a_sin.sem, 1)
                    own(tt(PT_[:, AQ + j, CTX:T], PT_[:, AQ + j, CTX:T], const(K_COS, LAT), ALU.mult))
                    tt(PT_[:, AQ + j, CTX:T], PT_[:, AQ + j, CTX:T], rt[:, j % 2, :], ALU.add).then_inc(a_rope.sem, 1)
                units, prods = attn_units(l)

                def negmax(u):
                    h, q, nk, _ = units[u]
                    dve.wait_ge(*a_s.at(l, u + 1))
                    if u >= 2:
                        dve.wait_ge(*a_exp.at(l, u - 1))
                    a = 2 * (u % 2)
                    if nk > 4:
                        src = PS[:, a:a + 2, :].rearrange("p b n -> p (b n)")[:, 0:nk * C]
                    else:
                        src = PS[:, a, 0:nk * C]
                    nc.vector.tensor_reduce(NEGM[:, u % 2:u % 2 + 1], src, AX.X, ALU.max, negate=True)\
                        .then_inc(a_max.sem, 1)

                def scaled(u):
                    h, q, nk, pr = units[u]
                    dve.wait_ge(*a_exp.at(l, u + 1))
                    own(nc.vector.reciprocal(PSUMS[:, 2 + u % 2:3 + u % 2], PSUMS[:, u % 2:u % 2 + 1]))
                    ts(Pb[:, u % 2, 0:nk * C], Pb[:, u % 2, 0:nk * C], PSUMS[:, 2 + u % 2:3 + u % 2], None, ALU.mult)\
                        .then_inc(a_scaled.sem, 1)

                def turned(u):
                    h, q, nk, pr = units[u]
                    q0 = prods[pr][1]
                    if u % 2 == 0:
                        return
                    dve.wait_ge(*a_T.at(l, u + 1))
                    if pr >= 2:
                        dve.wait_ge(*a_pv.at(l, pr - 1))
                    src = PS[:, 4:6, :].rearrange("p b n -> p (b n)")[:, 0:nk * C]
                    cp(PTr[:, pr % 2, 0:nk, (q - q0) * C:(q - q0) * C + C],
                       src.rearrange("p (k c) -> p k c", k=nk)).then_inc(a_Tdve.sem, 1)

                negmax(0)
                negmax(1)
                for u in range(len(units)):
                    scaled(u)
                    if u:
                        turned(u - 1)
                    if u + 2 < len(units):
                        negmax(u + 2)
                turned(len(units) - 1)

            for l in range(DEPTH):
                n_in, n_out, n_ff = slots(l)
                if l == 0:
                    low(0, 0)
                    dve.wait_ge(*wg_high.at(l, 1))
                    tt(wg_lo[:, :, :], wg_raw[:, :, :], wg_hi[:, :, :].bitcast(F32), ALU.subtract).then_inc(wg_low.sem, 1)
                if l == 0:
                    for k in range(DK):
                        sum_square(0, 0, k)
                u_parts(l, 0, SEGS)
                if l:
                    dve.wait_ge(*wg_high.at(l, 1))
                    tt(wg_lo[:, :, :], wg_raw[:, :, :], wg_hi[:, :, :].bitcast(F32), ALU.subtract).then_inc(wg_low.sem, 1)

                def tap(w, j):
                    return par(V_CONV + 12 * l + 4 * w + j)

                def beside(s):
                    if s == 8:
                        dve.wait_ge(*evac_act.at(l, 8))
                        if l:
                            dve.wait_ge(ctx_zero.sem, 4)
                    if 8 <= s < 12:
                        j = s - 8
                        y, p = Y[:, j, :], PT_[:, MQ + j, :]
                        own(ts(y, p, tap(1, j), None, ALU.mult))
                        for a, n in SEGS:
                            last = stt(y[:, a + 1:a + n], p[:, a:a + n - 1], tap(0, j), y[:, a + 1:a + n], ALU.mult, ALU.add)
                        own(last)
                        for a, n in SEGS:
                            last = stt(y[:, a:a + n - 1], p[:, a + 1:a + n], tap(2, j), y[:, a:a + n - 1], ALU.mult, ALU.add)
                        own(last)
                        ts(p, y, -41.0, None, ALU.max).then_inc(conv_done.sem, 1)
                    if 11 <= s < 15:
                        j = s - 11
                        dve.wait_ge(*ml_exp.at(l, j + 1))
                        stt(PT_[:, MQ + j, :], Y[:, j, :], 1.0 if j < 2 else HD ** -0.5, PT_[:, MQ + j, :], ALU.mult,
                            ALU.mult).then_inc((ml_q if j < 2 else ml_k).sem, 1)
                    if 17 <= s < 21:
                        q = s - 17
                        dve.wait_ge(*z_exp.at(l, q + 1))
                        ts(PT_[:, HZ + q, :], PT_[:, HZ + q, :], LB1[:, l, q:q + 1], LB[:, l, q:q + 1], ALU.mult, ALU.add)\
                            .then_inc(forget.sem, 1)

                for s in range(IN_TILES):
                    low(n_in + s + 1, s + 1)
                    beside(s)
                mlstm(l)
                hgrn(l)
                attention(l)
                dve.wait_ge(late_taken.sem, LATE_AFTER[l])
                for layer, m0, m1 in (((0, 16, 48), (1, 0, 16)), ((1, 16, 48),))[l]:
                    last = tt(MOD[:, layer, m0:m1, :], MOD[:, layer, m0:m1, :],
                              V[:, V_BMOD + 48 * layer + m0:V_BMOD + 48 * layer + m1].unsqueeze(2)
                              .broadcast_to([P, m1 - m0, 2]), ALU.add)
                own(last)
                if l == 0:
                    gains(1, 0)
                own(gains(l, 1))
                dve.memset(EPST[:, 1:2], 0.0).then_inc(late_ready.sem, 1)
                s0 = segs(l)[0][0]
                dve.wait_ge(*a_out.at(l, len(attn_units(l)[1])))
                for k in range(DK):
                    src = AO[:, k, s0:T] if k < 4 else PT_[:, (HQ if k < 6 else MO) + k % 2, s0:T]
                    dve.wait_ge(*u_high.at(l, 9 + k))
                    tt(Ul[:, k, s0:T], src, Uh[:, k, s0:T].bitcast(F32), ALU.subtract).then_inc(u_ready.sem, 1)

                def add_to_residual(j, gate_row, g=None):
                    for bank, (t0, tn) in enumerate(SEGS):
                        if (t0, tn) in segs(l):
                            who = 1 if t0 == 0 else 0
                            last = stt(H[:, j, t0:t0 + tn], PS[:, 2 * (j % 2) + bank, 0:tn],
                                       MOD[:, l, gate_row + j, who:who + 1], H[:, j, t0:t0 + tn], ALU.mult, ALU.add)
                    last.then_inc(evac_dve.sem, 1)

                for j in range(8):
                    low(n_out + j + 1, j + 1)
                    dve.wait_ge(gemm.sem, n_out + j + 1)
                    add_to_residual(j, 16)
                    if j:
                        sum_square(l, 1, j - 1)
                sum_square(l, 1, 7)
                dve.wait_ge(*evac_dve.at(l, 8))
                u_parts(l, 1, segs(l))

                def mlp(g, last_group=False):
                    for j in range(8):
                        low(n_ff + g * 16 + j + 1, j + 1)
                        t0 = segs(l)[0][0]
                        f = 32 * l + g * 8 + j
                        dve.wait_ge(evac_act.sem, 56 * l + 24 + g * 8 + j + 1)
                        if not isinstance(f, int) or f >= 2:
                            dve.wait_ge(hid_ready.sem, f - 1)
                        tt(hsq[:, j % 2, t0:T], relu[:, j % 2, t0:T], relu[:, j % 2, t0:T], ALU.mult)\
                            .then_inc(hid_square.sem, 1)
                        dve.wait_ge(hid_square.sem, f + 1)
                        dve.wait_ge(hid_high.sem, f + 1)
                        tt(hidl[:, j, t0:T], hsq[:, j % 2, t0:T], hidh[:, j, t0:T].bitcast(F32), ALU.subtract)\
                            .then_inc(hid_ready.sem, 1)
                    for j in range(8):
                        if not (last_group and l and j == 7):
                            low(n_ff + g * 16 + 8 + j + 1, j + 1)
                        dve.wait_ge(gemm.sem, n_ff + g * 16 + 8 + j + 1)
                        if j == 0:
                            dve.wait_ge(evac_dve.sem, 40 * l + 8 + g * 8)
                        add_to_residual(j, 40)
                        if last_group and l == 0 and j:
                            sum_square(l + 1, 0, j - 1)
                    if last_group and l == 0:
                        sum_square(l + 1, 0, 7)

                mlp(0)
                with dve.Fori(1, FG - 1) as g:
                    mlp(g)
                mlp(FG - 1, True)
            for i in range(4):
                dve.wait_ge(out_T.sem, 2 * i + 2)
                cp(onat[:, i, 512:1024], PS[:, 5 + 2 * (i % 2), :]).then_inc(out_dve.sem, 1)


_INS = ['x', 'c', 'ctx', 'c_ctx', 'w_mod', 'b_mod', 'norm_mix', 'norm_ffn', 'w_in', 'b_in', 'q_norm', 'k_norm',
        'hg_lb', 'hg_norm', 'ml_conv', 'w_out', 'w_ff1', 'w_ff2']


def kernel(**inputs):
    import numpy as _np
    import concourse.bacc as _bacc
    from concourse import mybir as _mybir
    from concourse.bass_utils import run_bass_kernel_spmd as _run

    nc = _bacc.Bacc("TRN2", target_bir_lowering=False, num_devices=1)
    arrays, args = {}, []
    k, m = tables()
    for name, a in [(n, inputs[n]) for n in _INS] + [("constants", k), ("level_masks", m)]:
        a = _np.ascontiguousarray(a)
        arrays[f"in_{name}_dram"] = a
        args.append(nc.dram_tensor(f"in_{name}_dram", a.shape, _mybir.dt.from_np(a.dtype), kind="ExternalInput").ap())
    args.append(nc.dram_tensor("out_0_dram", (1, LAT, D), F32, kind="ExternalOutput").ap())
    hybrid_dit_block(nc, *args)
    r = _run(nc, [arrays], core_ids=[0])
    return r.results[0]["out_0_dram"]
```
